# Optimizing a Trainium2 kernel written in Bass

```python
import math
import jax, jax.numpy as jnp
from jax import lax
import numpy as np

D_MODEL = 1024
BATCH = 1
SEQ = 512
DEPTH = 2
DEC_BATCH = 8
DEC_SEQ = 8
PAST_LEN = 1024
PAGE_SIZE = 128

N_A_LAYERS = DEPTH // 2
N_B_LAYERS = DEPTH - N_A_LAYERS
D_FF = 2816
CONV_WIDTH = 31
CONV_INNER = D_MODEL
GROUPS = ((128, 1), (512, 4), (2048, 16))
N_GROUPS = 3
HEADS_PER_GROUP = 8
HEAD_DIM = 64
ATTN_WIDTH = HEADS_PER_GROUP * HEAD_DIM
Q_WIDTH = N_GROUPS * ATTN_WIDTH
KV_WIDTH = N_GROUPS * 2 * ATTN_WIDTH
N_BUCKETS = 32
MAX_DISTANCE = 2048
QBLOCK = 128
EPS = 1e-6
NEG_INF = -1e30

kernel_name = "yoco_conformer_dilated_attn_step"

def rmsnorm(x, g):
    xf = x.astype(jnp.float32)
    y = xf * lax.rsqrt(jnp.mean(xf * xf, axis=-1, keepdims=True) + EPS)
    return (y * g.astype(jnp.float32)).astype(x.dtype)

def layernorm(x, g, b):
    xf = x.astype(jnp.float32)
    mu = jnp.mean(xf, axis=-1, keepdims=True)
    var = jnp.mean(jnp.square(xf - mu), axis=-1, keepdims=True)
    y = (xf - mu) * lax.rsqrt(var + EPS)
    return (y * g.astype(jnp.float32) + b.astype(jnp.float32)).astype(x.dtype)

def swiglu_ffn(h, w_in, w_out):
    gate, up = jnp.split(h @ w_in, 2, axis=-1)
    return (jax.nn.silu(gate) * up) @ w_out

def conformer_conv(h, prev, w_pw1, b_pw1, w_dw, b_dw, ln_g, ln_b, w_pw2, b_pw2):
    a, g = jnp.split(h @ w_pw1 + b_pw1, 2, axis=-1)
    u = a * jax.nn.sigmoid(g)
    u_ext = jnp.concatenate([prev.astype(u.dtype), u], axis=1)
    c = lax.conv_general_dilated(u_ext, w_dw[:, None, :].astype(u.dtype), window_strides=(1,),
                                 padding='VALID', dimension_numbers=('NWC', 'WIO', 'NWC'),
                                 feature_group_count=CONV_INNER) + b_dw
    c = jax.nn.silu(layernorm(c, ln_g, ln_b))
    return c @ w_pw2 + b_pw2, u_ext[:, -(CONV_WIDTH - 1):]

def t5_bucket(dist):
    max_exact = N_BUCKETS // 2
    d_f = jnp.maximum(dist, 1).astype(jnp.float32)
    large = max_exact + (jnp.log(d_f / max_exact) / math.log(MAX_DISTANCE / max_exact)
                         * (N_BUCKETS - max_exact)).astype(jnp.int32)
    large = jnp.minimum(large, N_BUCKETS - 1)
    return jnp.where(dist < max_exact, dist, large)

def group_bias(rel_bias, g):
    w, d = GROUPS[g]
    n_keys = w // d + 1
    dist = d * jnp.arange(n_keys, dtype=jnp.int32)
    b = jnp.take(rel_bias, t5_bucket(dist), axis=0)
    return b[:, g * HEADS_PER_GROUP:(g + 1) * HEADS_PER_GROUP].T.astype(jnp.float32)

def dilated_attend(q, k_ext, v_ext, q_idx, min_valid, dilation, n_keys, bias):
    offs = dilation * jnp.arange(n_keys, dtype=jnp.int32)
    idx = q_idx[:, None] - offs[None, :]
    valid = idx >= min_valid
    idx = jnp.maximum(idx, 0)
    kg = jnp.take(k_ext, idx, axis=1)
    vg = jnp.take(v_ext, idx, axis=1)
    logits = jnp.einsum('bthd,btnhd->bhtn', q, kg).astype(jnp.float32) * (HEAD_DIM ** -0.5)
    logits = logits + bias[None, :, None, :]
    logits = jnp.where(valid[None, None], logits, NEG_INF)
    m = jnp.max(logits, axis=-1, keepdims=True)
    p = jnp.exp(logits - m)
    den = jnp.sum(p, axis=-1, keepdims=True)
    o = jnp.einsum('bhtn,btnhd->bthd', (p / den).astype(v_ext.dtype), vg)
    lse = (m + jnp.log(den))[..., 0]
    return o, jnp.transpose(lse, (0, 2, 1))

def prompt_dilated(q, kv, g, bias):
    w, d = GROUPS[g]
    n_keys = w // d + 1
    B, S = q.shape[0], q.shape[1]
    kv_ext = jnp.concatenate([jnp.zeros((B, w) + kv.shape[2:], kv.dtype), kv], axis=1)
    k_ext, v_ext = kv_ext[:, :, 0], kv_ext[:, :, 1]
    nb = S // QBLOCK
    qb = jnp.swapaxes(q.reshape(B, nb, QBLOCK, HEADS_PER_GROUP, HEAD_DIM), 0, 1)
    ib = (w + jnp.arange(S, dtype=jnp.int32)).reshape(nb, QBLOCK)
    o, lse = lax.map(lambda a: dilated_attend(a[0], k_ext, v_ext, a[1], w, d, n_keys, bias), (qb, ib))
    o = jnp.swapaxes(o, 0, 1).reshape(B, S, HEADS_PER_GROUP, HEAD_DIM)
    lse = jnp.swapaxes(lse, 0, 1).reshape(B, S, HEADS_PER_GROUP)
    return o, lse

def sample_dilated(q, kv_new, buf, g, bias):
    w, d = GROUPS[g]
    n_keys = w // d + 1
    B, T = q.shape[0], q.shape[1]
    buf_len = buf.shape[1]
    kv_ext = jnp.concatenate([jnp.zeros((B, w) + kv_new.shape[2:], kv_new.dtype),
                              buf.astype(kv_new.dtype), kv_new], axis=1)
    k_ext, v_ext = kv_ext[:, :, 0], kv_ext[:, :, 1]
    q_idx = w + buf_len + jnp.arange(T, dtype=jnp.int32)
    min_valid = w + buf_len - PAST_LEN
    return dilated_attend(q, k_ext, v_ext, q_idx, min_valid, d, n_keys, bias)

def merge_groups(outs, lses):
    wts = jax.nn.softmax(jnp.stack(lses, axis=0), axis=0)
    return jnp.einsum('gbth,gbthd->bthd', wts.astype(outs[0].dtype), jnp.stack(outs, axis=0))

def trunk(x, conv_prev, kv_bufs, norms, ffn_w_in, ffn_w_out, conv_w_pw1, conv_b_pw1, conv_w_dw, conv_b_dw,
          conv_ln_g, conv_ln_b, conv_w_pw2, conv_b_pw2, norm_kv, w_kv, attn_w_q, attn_w_o, rel_bias, norm_final):
    B, T = x.shape[0], x.shape[1]
    biases = [group_bias(rel_bias, g) for g in range(N_GROUPS)]
    new_conv = []
    new_kv = []
    shared = None
    for li in range(DEPTH):
        x = x + 0.5 * swiglu_ffn(rmsnorm(x, norms[li, 0]), ffn_w_in[li, 0], ffn_w_out[li, 0])
        h = rmsnorm(x, norms[li, 1])
        if li < N_A_LAYERS:
            y, st = conformer_conv(h, conv_prev[li], conv_w_pw1[li], conv_b_pw1[li], conv_w_dw[li], conv_b_dw[li],
                                   conv_ln_g[li], conv_ln_b[li], conv_w_pw2[li], conv_b_pw2[li])
            new_conv.append(st)
        else:
            lb = li - N_A_LAYERS
            q = (h @ attn_w_q[lb]).reshape(B, T, N_GROUPS, HEADS_PER_GROUP, HEAD_DIM)
            outs, lses = [], []
            for g in range(N_GROUPS):
                if kv_bufs is None:
                    o, l = prompt_dilated(q[:, :, g], shared[:, :, g], g, biases[g])
                else:
                    o, l = sample_dilated(q[:, :, g], shared[:, :, g], kv_bufs[g], g, biases[g])
                outs.append(o)
                lses.append(l)
            y = merge_groups(outs, lses).reshape(B, T, ATTN_WIDTH) @ attn_w_o[lb]
        x = x + y
        x = x + 0.5 * swiglu_ffn(rmsnorm(x, norms[li, 2]), ffn_w_in[li, 1], ffn_w_out[li, 1])
        if li == N_A_LAYERS - 1:
            shared = (rmsnorm(x, norm_kv) @ w_kv).reshape(B, T, N_GROUPS, 2, HEADS_PER_GROUP, HEAD_DIM)
            for g in range(N_GROUPS):
                kv_g = shared[:, :, g]
                if kv_bufs is None:
                    keep = min(GROUPS[g][0], T)
                    new_kv.append(kv_g[:, T - keep:])
                else:
                    buf_len = kv_bufs[g].shape[1]
                    new_kv.append(jnp.concatenate([kv_bufs[g].astype(kv_g.dtype), kv_g], axis=1)[:, -buf_len:])
    return rmsnorm(x, norm_final), jnp.stack(new_conv, axis=0), new_kv

def setup_inputs(seed: int = 0) -> dict:
    key = jax.random.key(seed)
    ks = jax.random.split(key, 24)

    def nrm(k, shape, scale):
        return jax.random.normal(k, shape, jnp.float32) * scale

    def buf(w):
        return min(w, PAST_LEN)

    kvshape = (2, HEADS_PER_GROUP, HEAD_DIM)
    return {
        "x_prompt": nrm(ks[0], (BATCH, SEQ, D_MODEL), 1.0),
        "x_sample": nrm(ks[1], (DEC_BATCH, DEC_SEQ, D_MODEL), 1.0),
        "state_conv": nrm(ks[2], (N_A_LAYERS, DEC_BATCH, CONV_WIDTH - 1, CONV_INNER), 0.5),
        "cache_kv_w128": nrm(ks[3], (DEC_BATCH, buf(GROUPS[0][0])) + kvshape, 1.0),
        "cache_kv_w512": nrm(ks[4], (DEC_BATCH, buf(GROUPS[1][0])) + kvshape, 1.0),
        "cache_kv_w2048": nrm(ks[5], (DEC_BATCH, buf(GROUPS[2][0])) + kvshape, 1.0),
        "norms": 1.0 + nrm(ks[6], (DEPTH, 3, D_MODEL), 0.02),
        "ffn_w_in": nrm(ks[7], (DEPTH, 2, D_MODEL, 2 * D_FF), D_MODEL ** -0.5),
        "ffn_w_out": nrm(ks[8], (DEPTH, 2, D_FF, D_MODEL), D_FF ** -0.5),
        "conv_w_pw1": nrm(ks[9], (N_A_LAYERS, D_MODEL, 2 * CONV_INNER), D_MODEL ** -0.5),
        "conv_b_pw1": nrm(ks[10], (N_A_LAYERS, 2 * CONV_INNER), 0.02),
        "conv_w_dw": nrm(ks[11], (N_A_LAYERS, CONV_WIDTH, CONV_INNER), CONV_WIDTH ** -0.5),
        "conv_b_dw": nrm(ks[12], (N_A_LAYERS, CONV_INNER), 0.02),
        "conv_ln_g": 1.0 + nrm(ks[13], (N_A_LAYERS, CONV_INNER), 0.02),
        "conv_ln_b": nrm(ks[14], (N_A_LAYERS, CONV_INNER), 0.02),
        "conv_w_pw2": nrm(ks[15], (N_A_LAYERS, CONV_INNER, D_MODEL), CONV_INNER ** -0.5),
        "conv_b_pw2": nrm(ks[16], (N_A_LAYERS, D_MODEL), 0.02),
        "norm_kv": 1.0 + nrm(ks[17], (D_MODEL,), 0.02),
        "w_kv": nrm(ks[18], (D_MODEL, KV_WIDTH), D_MODEL ** -0.5),
        "attn_w_q": nrm(ks[19], (N_B_LAYERS, D_MODEL, Q_WIDTH), D_MODEL ** -0.5),
        "attn_w_o": nrm(ks[20], (N_B_LAYERS, ATTN_WIDTH, D_MODEL), ATTN_WIDTH ** -0.5),
        "rel_bias": nrm(ks[21], (N_BUCKETS, N_GROUPS * HEADS_PER_GROUP), 0.5),
        "norm_final": 1.0 + nrm(ks[22], (D_MODEL,), 0.02),
    }

def reference(x_prompt, x_sample, state_conv, cache_kv_w128, cache_kv_w512, cache_kv_w2048, norms, ffn_w_in,
              ffn_w_out, conv_w_pw1, conv_b_pw1, conv_w_dw, conv_b_dw, conv_ln_g, conv_ln_b, conv_w_pw2, conv_b_pw2,
              norm_kv, w_kv, attn_w_q, attn_w_o, rel_bias, norm_final):
    zeros_conv = jnp.zeros((N_A_LAYERS, x_prompt.shape[0], CONV_WIDTH - 1, CONV_INNER), x_prompt.dtype)
    y_prompt, conv_prompt, kv_prompt = trunk(
        x_prompt, zeros_conv, None, norms, ffn_w_in, ffn_w_out, conv_w_pw1, conv_b_pw1, conv_w_dw, conv_b_dw,
        conv_ln_g, conv_ln_b, conv_w_pw2, conv_b_pw2, norm_kv, w_kv, attn_w_q, attn_w_o, rel_bias, norm_final)
    y_sample, conv_sample, kv_sample = trunk(
        x_sample, state_conv, (cache_kv_w128, cache_kv_w512, cache_kv_w2048), norms, ffn_w_in, ffn_w_out,
        conv_w_pw1, conv_b_pw1, conv_w_dw, conv_b_dw, conv_ln_g, conv_ln_b, conv_w_pw2, conv_b_pw2, norm_kv, w_kv,
        attn_w_q, attn_w_o, rel_bias, norm_final)
    kv128_prompt, kv512_prompt, kv2048_prompt = kv_prompt
    kv128_sample, kv512_sample, kv2048_sample = kv_sample
    return (y_prompt, y_sample, conv_prompt, conv_sample, kv128_prompt, kv128_sample,
            kv512_prompt, kv512_sample, kv2048_prompt, kv2048_sample)


_drawn_inputs = setup_inputs


def setup_inputs(seed=0):
    import zlib

    import numpy as np

    out = dict(_drawn_inputs(seed))
    spreads = {}
    factors = {'conv_ln_g': 4.029,
     'conv_ln_b': 4.637,
     'conv_b_pw2': 2.859,
     'norm_kv': 8.162,
     'norm_final': 8.045}
    for name, (base, spread) in spreads.items():
        noise = np.random.default_rng([zlib.crc32(name.encode()), seed]).standard_normal(out[name].shape)
        drawn = base * np.exp(spread * noise) if base else spread * noise
        out[name] = __import__('jax').numpy.asarray(drawn.astype(out[name].dtype))
    for name, factor in factors.items():
        out[name] = (out[name] * factor).astype(out[name].dtype)
    return out
```

```python
import concourse.bass as bass
from concourse import mybir
import numpy as np

f32, f32r = mybir.dt.float32, mybir.dt.float32r
ALU, ACT, AX = mybir.AluOpType, mybir.ActivationFunctionType, mybir.AxisListType

P = 128
D, FF, SEQ, NB, NT = 1024, 2816, 512, 8, 8
SMP = NB * NT
TOK = SEQ + SMP
HALF = TOK // 2
KD, KF = D // P, FF // P
CW = 31
CD = 5
CP = KD - CD
HEADS, HD, AW = 8, 64, 512
PAIRS = HEADS * HD // P
WIN, DIL = (128, 512, 2048), (1, 4, 16)
CACHE = (128, 512, 1024)
EPS = 1e-6
NEG = -1e30
SLOT = KF // 2 * P
TT = 5

NORM, NORM_KV, NORM_F, B_PW1, B_DW, LN_G, LN_B, B_PW2, W_DW = 0, 6, 7, 8, 10, 11, 12, 13, 14
NPAR = W_DW + CW

R0_LEN = 4 * (P - 1) + SEQ + 3
R1_LEN = 2 * P - 1
R_LEN = R0_LEN + 2 * R1_LEN
T0W = SEQ + 3
C1, C2, C0, CN = 0, 512, 1024, 1152
SC = CN + 3 * NT

_W_PHASES = ("ffn0_in", "ffn0_out", "pw1", "pw2", "ffn1_in", "ffn1_out", "kv", "ffn2_in", "ffn2_out",
             "q", "wo", "ffn3_in", "ffn3_out")
CHUNKS = dict(pw1=16, pw2=8, kv=24, q=12, wo=4, **{f"ffn{n}_in": 2 * KF for n in range(4)},
              **{f"ffn{n}_out": 2 * KD for n in range(4)})
SIZE = dict(pw1=8 * P, pw2=8 * P, kv=8 * P, q=8 * P, wo=8 * P, **{f"ffn{n}_in": 8 * P for n in range(4)},
            **{f"ffn{n}_out": SLOT for n in range(4)})
MTILES = dict(pw1=16, pw2=0, kv=0, q=12, wo=0, **{f"ffn{n}_in": 2 * KF for n in range(4)},
              **{f"ffn{n}_out": 0 for n in range(4)})
CB = {ph: sum(CHUNKS[x] for x in _W_PHASES[:n]) for n, ph in enumerate(_W_PHASES)}
MB = {ph: sum(MTILES[x] for x in _W_PHASES[:n]) for n, ph in enumerate(_W_PHASES)}
NEXT_SIZE = {ph: SIZE[nx] for ph, nx in zip(_W_PHASES, _W_PHASES[1:])}
NEXT_SIZE[_W_PHASES[-1]] = None


def bucket(dist):
    d = np.maximum(dist, 1).astype(np.float32)
    large = 16 + (np.log(d / np.float32(16)) / np.float32(np.log(2048 / 16)) * 16).astype(np.int32)
    return np.where(dist < 16, dist, np.minimum(large, 31))


def bias_onehots():
    one = np.zeros((33, R_LEN), np.float32)

    def put(col, ok, dist):
        one[np.where(ok, bucket(np.where(ok, dist, 0)), 32), col] = 1.0

    y = np.arange(R0_LEN)
    n = SEQ - 1 - y
    put(y, (n >= 0) & (n <= WIN[0]), n)
    y = np.arange(R1_LEN)
    n = P - 1 - y
    put(R0_LEN + y, n >= 0, 4 * n)
    put(R0_LEN + R1_LEN + y, (n >= 0) & (n % 4 == 0), 4 * n)
    hot, bad = np.zeros((2, P, SC), np.float32), np.zeros((NT, SC), np.float32)
    for t in range(NT):
        dist = np.full(SC, -1)
        p = np.arange(CACHE[1])
        dist[C1:C2] = np.where((CACHE[1] + t - p) % DIL[1] == 0, CACHE[1] + t - p, -1)
        m, tt = np.arange(512) // 8, np.arange(512) % 8
        dist[C2:C0] = np.where(tt == t, PAST - 16 * m, -1)
        dist[C0:CN] = CACHE[0] + t - np.arange(P)
        for g in range(3):
            lag = t - np.arange(NT)
            dist[CN + g:SC:3] = np.where((lag >= 0) & (lag % DIL[g] == 0), lag, -1)
        top = np.full(SC, WIN[0])
        top[C1:C2], top[C2:C0] = WIN[1], WIN[2]
        ok = (dist >= 0) & (dist <= top)
        c = np.arange(SC)[ok]
        hot[t // 4, 32 * (t % 4) + bucket(dist[ok]), c] = 1.0
        bad[t, ~ok] = 1.0
    rows = np.zeros((NT, P), np.float32)
    for t in range(NT):
        for j in range(PAIRS):
            rows[t, [32 * j + t, 32 * j + NT + t]] = NEG
    return one, hot, bad, rows


PAST = 1024


class Steps:

    def __init__(self, engine, sem):
        self.engine, self.sem, self.n, self.i, self.per = engine, sem, 0, None, 0

    def mark(self, instruction):
        instruction.then_inc(self.sem, 1)
        self.n += 1

    def wait(self, back=0):
        at = self.n - back
        self.engine.wait_ge(self.sem, at if self.i is None else self.i * self.per + at)

    def loop(self, i, per):
        self.i, self.per, self.start = i, per, self.n

    def end(self, times):
        assert self.n - self.start == self.per, (self.n - self.start, self.per)
        self.n, self.i = self.start + self.per * times, None


def trunk_program(nc, I, O):
    sb0 = (nc.sbuf_usable_end - nc.sbuf_bytes_remaining + 63) // 64 * 64
    at = [sb0]

    def place(name, shape, dt=f32):
        t = nc.alloc_sbuf_tensor_at(name, shape, dt, offset=at[0])
        at[0] += (int(np.prod(shape[1:])) * 4 + 31) // 32 * 32
        return t

    xT = place("xT", [P, KD, 2, HALF])
    hH = place("hH", [P, KD, 2, HALF], f32r)
    hL = place("hL", [P, KD, 2, HALF], f32r)
    wst = place("wst", [P, 4, SLOT])
    wH = place("wH", [P, 2, SLOT], f32r)
    wL = place("wL", [P, 2, SLOT], f32r)
    rstd = place("rstd", [P, 2, HALF])
    par = place("par", [P, KD, NPAR])
    ident = place("ident", [P, P])
    ones = place("ones", [P, P])
    ta = place("ta", [P, 2, HALF])
    tb = place("tb", [P, 2, HALF])
    eps = place("eps", [P, 1])
    rstdT = place("rstdT", [P, 8])
    void = place("void", [P, 1])
    A0 = at[0]

    def region(*what):
        at[0] = A0
        got = [place(*w) for w in what]
        assert at[0] <= A_END, (what, at[0] - A0)
        return got

    A_END = nc.sbuf_usable_end
    actH, actL = region(("actH", [P, KF, 2, HALF], f32r), ("actL", [P, KF, 2, HALF], f32r))
    xr, parR, relE, relq, E1, E2, Ebad, sel, selm, Rsb, sbias0 = region(
        ("xr", [P, TT, D]), ("parR", [NPAR, D]), ("relE", [33, 24]), ("relq", [P, 24]), ("E1", [33, R_LEN]),
        ("E2", [P, 2, SC]), ("Ebad", [NT, SC]), ("sel", [P, 2, 3, P]), ("selm", [NT, P]), ("Rsb", [24, R_LEN]),
        ("sbias0", [P, SC]))
    UW = 30 + SEQ + NB * (30 + NT)
    wdH, wdL, stR, ucat, cT, cst, un, cH, cL = region(
        ("wdH", [P, CP, CW], f32r), ("wdL", [P, CP, CW]),
        ("stR", [120, 2, D]), ("ucat", [P, KD, UW]), ("cT", [P, KD, 2, HALF]), ("cst", [SMP, 2, D]),
        ("un", [P, KD, SMP]), ("cH", [P, KD, 2, HALF], f32r), ("cL", [P, KD, 2, HALF], f32r))
    c_end = at[0]
    at[0] = A0 + 2 * 384
    tS = place("tS", [P, 2, 4 * SMP])
    diagH, diagL, uH, uL = [], [], [], []
    for slot, base in enumerate((c_end - 2 * KD * TOK * 4, sb0 + KD * TOK * 4)):
        at[0] = base
        diagH.append(place(f"diagH{slot}", [P, CW, P], f32r))
        diagL.append(place(f"diagL{slot}", [P, CW, P], f32r))
        uH.append(place(f"uH{slot}", [P, 30 + SEQ], f32r))
        uL.append(place(f"uL{slot}", [P, 30 + SEQ], f32r))
    kvst, = region(("kvst", [P, 2, TT, AW]))
    qT, oT, kin, vin, bT, qc, kT, sP, pT, oS, stat = region(
        ("qT", [P, 12, TOK]), ("oT", [P, PAIRS, 2, HALF]), ("kin", [P, 12, P]), ("vin", [P, 12, P]),
        ("bT", [P, 2, T0W + 2 * P]), ("qc", [P, 3, 4, P]), ("kT", [P, 3, SEQ]), ("sP", [P, 2, 768]),
        ("pT", [P, 2, 768]), ("oS", [P, 4, P]), ("stat", [P, 32]))
    at[0] = A0 + (12 * TOK + PAIRS * TOK) * 4
    kc, vc = place("kc", [P, 9, AW]), place("vc", [P, 9, AW])
    qs, kn, vn, stS = place("qs", [P, 12, 32]), place("kn", [24, AW]), place("vn", [24, AW]), place("stS", [P, 4])
    assert at[0] <= A_END
    oH, oL = region(("oH", [P, PAIRS, 2, HALF], f32r), ("oL", [P, PAIRS, 2, HALF], f32r))
    H0 = sb0 + KD * TOK * 4
    at[0] = H0
    kTs, sS, ptS, sbias = (place("kTs", [P, PAIRS, SC]), place("sS", [P, SC]), place("ptS", [P, 10, P]),
                           place("sbias", [P, SC]))
    assert at[0] <= H0 + 2 * KD * TOK * 4
    at[0] = H0
    yg, yst = place("yg", [P, KD, 2, HALF]), place("yst", [P, 2, D])
    assert at[0] <= H0 + 2 * KD * TOK * 4

    ps = nc.alloc_psum_tensor("ps", [P, 8, 512], f32)

    def pair(p):
        return ps[:, 2 * p:2 * p + 2, 0:HALF]

    def tile(t, k):
        return t[:, k] if isinstance(k, int) else t[:, bass.ds(k, 1)].rearrange("p o a b -> p (o a) b")

    def tokens(t, k=None):
        return (t[:] if k is None else tile(t, k)).rearrange("p a b -> p (a b)")

    def column(k, row):
        return par[:, k:k + 1, row] if isinstance(k, int) else par[:, bass.ds(k, 1), row]

    rvec = nc.dram_tensor("rvec", (24, R_LEN), f32, kind="Internal").ap()
    sbd = nc.dram_tensor("sbd", (P, SC), f32, kind="Internal").ap()
    kvs = nc.dram_tensor("kvs", (TOK, 6 * AW), f32, kind="Internal").ap()
    kvs3 = kvs.rearrange("t (g x) -> (t g) x", g=3)

    names = """par_in x_in bias_in st_in rvec_out sbd_out sbias_in kv_out0 kv_out1 kv_copy cache_copy state_copy
        conv_out y_out w_h w_ready pe_chunk wo_even evac x_ready h_h h_ready sq_ready ss_done std_ready ssT_done
        stdT_ready silu_done act_in act_h act_ready ident_ready consts_ready par_t par_ready x_t b_mm b_ev sel_ready
        glu_done st_t st_ready u_ready u_t u_ev c_ready mu_mm cc_ready csq_ready var_mm lnstd_ready ln_in
        kv_evac wd_h wd_ready diag_h diag_l uh_ready ul_ready ul7_ready conv_mm cp_ready cs_ready un_ready q_ready k_in v_in b_in kt_tr kt_d kt_a qc_ready s_done s_evac sm_ready p_ready pt_done pt_ready
        pv_done o_evac ot_done ot_ready kc_in vc_in ktr ktd kta ss_mm sm2 p2 pn ptr_d ptr_a ptr_mm pv2 o2
        yg_ready yt y_ready dve_self act_self pool_self""".split()
    S = {n: nc.alloc_semaphore(n) for n in names}
    w_in = [nc.alloc_semaphore(f"w_in{s}") for s in range(4)]

    FB = {f"ffn{n}_in": KF * n for n in range(4)}
    HB, hn = {}, 0
    for name, k in (("ffn0_in", 8), ("pw1", 8), ("pw2", 8), ("ffn1_in", 8), ("kv", 8), ("ffn2_in", 8), ("q", 8),
                    ("wo", 4), ("ffn3_in", 8)):
        HB[name] = hn
        hn += k
    XV = dict(ffn0_in=0, pw1=1, ffn1_in=2, kv=3, ffn2_in=3, q=4, ffn3_in=5, final=6)
    GAIN = dict(ffn0_in=NORM, pw1=NORM + 1, ffn1_in=NORM + 2, kv=NORM_KV, ffn2_in=NORM + 3, q=NORM + 4,
                ffn3_in=NORM + 5, final=NORM_F)
    AFTER = dict(ffn0_out="pw1", pw2="ffn1_in", ffn1_out="kv", ffn2_out="q", wo="ffn3_in", ffn3_out="final")
    ROUND = dict(ffn0_in=1, pw1=2, ffn1_in=3, ffn2_in=4, q=5, ffn3_in=6)
    ROUNDT = dict(kv=1, final=2)

    block_cm = nc.Block()
    block = block_cm.__enter__()

    w_view = {}
    for n in range(4):
        w_view[f"ffn{n}_in"] = I["ffn_w_in"][n // 2, n % 2].rearrange("(k p) n -> p k n", p=P)
        w_view[f"ffn{n}_out"] = I["ffn_w_out"][n // 2, n % 2].rearrange("(k p) n -> p k n", p=P)
    w_view["pw1"] = I["conv_w_pw1"][0].rearrange("(k p) n -> p k n", p=P)
    w_view["pw2"] = I["conv_w_pw2"][0].rearrange("(k p) n -> p k n", p=P)
    w_view["kv"] = I["w_kv"].rearrange("(k p) n -> p k n", p=P)
    w_view["q"] = I["attn_w_q"][0].rearrange("(k p) n -> p k n", p=P)
    w_view["wo"] = I["attn_w_o"][0].rearrange("(k p) n -> p k n", p=P)

    def chunk_source(sp, ph, i, s):
        w = w_view[ph]

        def at_col(x):
            return x if isinstance(x, int) else sp.snap(x)

        if ph.endswith("_in") or ph == "pw1":
            half = FF if ph != "pw1" else D
            return w[:, :, bass.ds(at_col(i * 2 * P + s // 2 * P + s % 2 * half), P)]
        if ph.endswith("_out"):
            return w[:, s % 2 * (KF // 2):(s % 2 + 1) * (KF // 2), bass.ds(at_col(i * 2 * P + s // 2 * P), P)]
        if ph in ("pw2", "q"):
            return w[:, :, bass.ds(at_col(i * 4 * P + s * P), P)]
        if ph == "kv":
            return w[:, 2 * s:2 * s + 2, bass.ds(at_col(i * AW), AW)]
        return w[:, :, bass.ds(at_col(i * 8 * P + s * 2 * P), 2 * P)]

    @block.sync
    def _(sp):
        sp.dma_start(parR[NORM:NORM + 6, :], I["norms"].rearrange("a b n -> (a b) n")).then_inc(S["par_in"], 16)
        sp.dma_start(parR[NORM_KV:NORM_KV + 1, :], I["norm_kv"][None, :]).then_inc(S["par_in"], 16)
        sp.dma_start(parR[NORM_F:NORM_F + 1, :], I["norm_final"][None, :]).then_inc(S["par_in"], 16)
        sp.dma_start(parR[B_PW1:B_PW1 + 2, :], I["conv_b_pw1"].rearrange("a (b n) -> (a b) n", b=2)
                     ).then_inc(S["par_in"], 16)
        for row, name in ((B_DW, "conv_b_dw"), (LN_G, "conv_ln_g"), (LN_B, "conv_ln_b"), (B_PW2, "conv_b_pw2")):
            sp.dma_start(parR[row:row + 1, :], I[name]).then_inc(S["par_in"], 16)
        sp.dma_start(parR[W_DW:NPAR, :], I["conv_w_dw"][0]).then_inc(S["par_in"], 16)
        sp.dma_start(xr[:, 0:4, :], I["x_prompt"][0].rearrange("(k p) n -> p k n", p=P)).then_inc(S["x_in"], 16)
        sp.dma_start(xr[0:SMP, 4, :], I["x_sample"].rearrange("b t n -> (b t) n")).then_inc(S["x_in"], 16)

        def chunk(ph, i, s, first=False):
            src = chunk_source(sp, ph, i, s)
            if not first:
                sp.wait_ge(S["w_ready"], i * 4 + (CB[ph] + s - 3))
            k, n = src.shape[1], src.shape[2]
            sp.dma_start(wst[:, s, 0:k * n].rearrange("p (k n) -> p k n", n=n), src).then_inc(w_in[s], 16)

        for s in range(4):
            chunk("ffn0_in", 0, s, first=True)
        sp.dma_start(relE[0:32, :], I["rel_bias"]).then_inc(S["bias_in"], 16)
        for q in range(4):
            sp.dma_start(relq[32 * q:32 * q + 32, :], I["rel_bias"]).then_inc(S["bias_in"], 16)
        sp.dma_start(E1[:], I["onehot"]).then_inc(S["bias_in"], 16)
        sp.dma_start(E2[:], I["onehot_sample"].rearrange("h p c -> p h c")).then_inc(S["bias_in"], 16)
        sp.dma_start(Ebad[:], I["unseen_sample"]).then_inc(S["bias_in"], 16)
        sp.dma_start(selm[:], I["unseen_rows"]).then_inc(S["bias_in"], 16)
        sp.wait_ge(S["b_ev"], 6)
        sp.dma_start(rvec, Rsb[:]).then_inc(S["rvec_out"], 16)
        sp.dma_start(sbd, sbias0[:]).then_inc(S["sbd_out"], 16)

        def stream(ph, start=0):
            n = CHUNKS[ph] // 4
            if n - start == 1:
                for s in range(4):
                    chunk(ph, start, s)
            else:
                with sp.Fori(start, n) as i:
                    for s in range(4):
                        chunk(ph, i, s)

        stream("ffn0_in", 1)
        stream("ffn0_out")
        for s in range(4):
            chunk("pw1", 0, s)
        sp.wait_ge(S["pe_chunk"], CB["pw1"])
        sp.dma_start(stR[:], I["state_conv"][0].rearrange("(h b) t n -> (b t) h n", h=2)).then_inc(S["st_in"], 16)
        stream("pw1", 1)
        for ph in ("pw2", "ffn1_in", "ffn1_out", "kv", "ffn2_in", "ffn2_out", "q", "wo"):
            stream(ph)
        sp.wait_ge(S["rvec_out"], 16)
        sp.wait_ge(S["sbd_out"], 16)
        sp.wait_ge(S["kv_out0"], 16 * 6)
        sp.wait_ge(S["kv_out1"], 16 * 6)
        sp.wait_ge(S["pe_chunk"], CB["q"])
        rt = rvec.tensor
        for j in range(PAIRS):
            if j:
                sp.wait_ge(S["kt_tr"], j)
            for g in range(3):
                for kv, dst, sem in ((0, kin, "k_in"), (1, vin, "v_in")):
                    if kv and j and not g:
                        sp.wait_ge(S["pv_done"], 8 * j)
                    src = kvs[0:SEQ, (2 * g + kv) * AW + j * P:(2 * g + kv) * AW + (j + 1) * P]
                    src = src.rearrange("(k p) n -> p k n", p=P) if g == 0 else src.rearrange("(a r) n -> a r n", r=4)
                    sp.dma_start(dst[:, 4 * g:4 * g + 4, :], src).then_inc(S[sem], 16)
            if j:
                sp.wait_ge(S["s_evac"], 1 + 8 * j)
            for h2 in range(2):
                h = 2 * j + h2
                for g, (off, step, col, n) in enumerate(((0, 4, 0, T0W), (R0_LEN, 1, T0W, P),
                                                         (R0_LEN + R1_LEN, 1, T0W + P, P))):
                    src = bass.AP(rt, (8 * g + h) * R_LEN + off, [[step, P], [1, n]])
                    sp.dma_start(bT[:, h2, col:col + n], src).then_inc(S["b_in"], 16)
        sp.wait_ge(S["pe_chunk"], CB["wo"])
        sp.dma_start(sbias[:], sbd).then_inc(S["sbias_in"], 16)
        sp.wait_ge(S["ot_ready"], PAIRS)
        c512 = I["cache_kv_w512"].rearrange("b (k p) v h d -> b p k v (h d)", p=P)
        c128 = I["cache_kv_w128"].rearrange("b p v h d -> b p v (h d)")
        c2048 = I["cache_kv_w2048"].rearrange("b (k m t) v h d -> b k m t v (h d)", k=4, t=16)
        for b in range(NB):
            for kv, dst, new, sem in ((0, kc, kn, "kc_in"), (1, vc, vn, "vc_in")):
                if b and kv == 0:
                    sp.wait_ge(S["ktr"], 12 * b)
                if b and kv == 1:
                    sp.wait_ge(S["pv2"], b)
                sp.dma_start(dst[:, 0:4, :], c512[b, :, :, kv, :]).then_inc(S[sem], 16)
                for k in range(4):
                    sp.dma_start(dst[:, 4 + k, :],
                                 c2048[b, k, :, 0:NT, kv, :]).then_inc(S[sem], 16)
                sp.dma_start(dst[:, 8, :], c128[b, :, kv, :]).then_inc(S[sem], 16)
                r0 = (SEQ + NT * b) * 3
                sp.dma_start(new[:], kvs3[r0:r0 + 24, kv * AW:(kv + 1) * AW]).then_inc(S[sem], 16)
        stream("ffn3_in")
        stream("ffn3_out")
        sp.wait_ge(S["kv_copy"], 16 * 6)
        sp.wait_ge(S["cache_copy"], 16 * 24)
        sp.wait_ge(S["state_copy"], 16)
        sp.wait_ge(S["conv_out"], 16 * 9)
        for t in range(TT):
            sp.wait_ge(S["y_ready"], t + 1)
            if t < 4:
                sp.dma_start(O["y_prompt"][0, t * P:(t + 1) * P, :], yst[:, t % 2, :]).then_inc(S["y_out"], 16)
            else:
                sp.dma_start(O["y_sample"].rearrange("b t n -> (b t) n"), yst[0:SMP, t % 2, :]
                             ).then_inc(S["y_out"], 16)
            sp.wait_ge(S["y_out"], 16 * (t + 1))

    @block.gpsimd
    def _(pool):
        me = Steps(pool, S["pool_self"])
        me.mark(nc.gpsimd.memset(ident[:], 0.0))
        me.wait()
        nc.gpsimd.affine_select(out=ident[:], in_=ident[:], compare_op=ALU.not_equal, fill=1.0, base=0,
                                pattern=[[-1, P]], channel_multiplier=1).then_inc(S["ident_ready"], 1)

        def squares(version):
            for k in range(KD):
                pool.wait_ge(S["x_ready"], KD * version + k + 1)
                if k == 0:
                    me.mark(nc.gpsimd.tensor_tensor(tokens(tb), tokens(xT, k), tokens(xT, k), ALU.mult))
                    continue
                me.mark(nc.gpsimd.tensor_tensor(tokens(ta), tokens(xT, k), tokens(xT, k), ALU.mult))
                me.wait()
                add = nc.gpsimd.tensor_tensor(tokens(tb), tokens(tb), tokens(ta), ALU.add)
                if k < KD - 1:
                    me.mark(add)
                    me.wait()
                else:
                    add.then_inc(S["sq_ready"], 1)

        def shift_cache(g, entries=range(NB), ph=None, start=0, every=0):
            for at_, b in enumerate(entries):
                if ph:
                    pool.wait_ge(S["pe_chunk"], CB[ph] + start + at_ * every)
                n = CACHE[g] - NT
                src = I[f"cache_kv_w{WIN[g]}"][b, NT:CACHE[g]].rearrange("t v h d -> t (v h d)")
                dst = O[f"kv{g}_sample"][b, 0:n].rearrange("t v h d -> t (v h d)")
                pool.dma_start(dst, src).then_inc(S["cache_copy"], 16)

        pool.wait_ge(S["consts_ready"], 1)
        squares(0)
        shift_cache(2, range(0, 4), "ffn0_in", 8, 10)
        squares(1)
        shift_cache(0, ph="pw1", start=1)
        pool.dma_start(O["conv_sample"][0, :, 0:CW - 1 - NT], I["state_conv"][0, :, NT:]).then_inc(S["state_copy"], 16)

        def diag_low(n):
            nc.gpsimd.tensor_tensor(diagL[n % 2][:], ident[:].rearrange("p (o c) -> p o c", o=1).broadcast_to([P, CW, P]),
                                    wdL[:, n, :].rearrange("p (k o) -> p k o", o=1).broadcast_to([P, CW, P]),
                                    ALU.mult).then_inc(S["diag_l"], 1)

        def u_low(n):
            pool.wait_ge(S["uh_ready"], n + 1)
            nc.gpsimd.tensor_tensor(uL[n % 2][:], ucat[:, CD + n, 0:30 + SEQ], uH[n % 2][:].bitcast(f32),
                                    ALU.subtract).then_inc(S["ul_ready"], 1)

        def sample_taps(q):
            tiles = slice(4 * q, 4 * q + 4)
            u4 = ucat[:, tiles, 30 + SEQ:UW].rearrange("p k (b t) -> p k b t", b=NB)
            c = cT[:, tiles].rearrange("p k a b -> p k (a b)")[:, :, SEQ:TOK]

            def row(r):
                return par[:, tiles, r:r + 1].rearrange("p k (x y) -> p k x y", y=1).broadcast_to([P, 4, NB, NT])

            def product(k):
                me.mark(nc.gpsimd.tensor_tensor(tS[:, k % 2, :].rearrange("p (k b t) -> p k b t", k=4, b=NB),
                                                u4[:, :, :, k:k + NT], row(W_DW + k), ALU.mult))

            def term(k):
                return tS[:, k % 2, :].rearrange("p (k x) -> p k x", k=4)

            pool.wait_ge(S["u_ready"], 4 * q + 4)
            if q:
                pool.wait_ge(S["cs_ready"], q)
            product(0)
            for k in range(CW):
                if k < CW - 1:
                    if k:
                        me.wait()
                    product(k + 1)
                if k == 0:
                    me.wait(1)
                    nx = nc.gpsimd.tensor_tensor(
                        c, term(0), par[:, tiles, B_DW:B_DW + 1].broadcast_to([P, 4, SMP]), ALU.add)
                else:
                    me.wait(1 if k < CW - 1 else 0)
                    nx = nc.gpsimd.tensor_tensor(c, c, term(k), ALU.add)
                if k < CW - 1:
                    me.mark(nx)
                else:
                    nx.then_inc(S["cs_ready"], 1)

        pool.wait_ge(S["pe_chunk"], CB["pw1"])
        pool.wait_ge(S["wd_ready"], 1)
        diag_low(0)
        pool.wait_ge(S["st_ready"], KD)
        sample_taps(0)
        u_low(0)
        pool.wait_ge(S["pe_chunk"], CB["pw2"])
        diag_low(1)
        u_low(1)
        sample_taps(1)
        for b in range(NB):
            if b == 0:
                pool.wait_ge(S["u_ev"], 4)
                pool.dma_start(O["conv_prompt"][0, 0], cst[0:30, 0, :]).then_inc(S["conv_out"], 16)
            pool.dma_start(O["conv_sample"][0, b, CW - 1 - NT:], cst[b * NT:(b + 1) * NT, 1, :]
                           ).then_inc(S["conv_out"], 16)
        squares(2)
        shift_cache(2, range(4, 8), "ffn1_in", 4, 10)
        squares(3)
        for n in range(6):
            pool.wait_ge(S["kv_evac"], 5 * n + 10)
            cols = slice(n * AW, (n + 1) * AW)
            out = S[f"kv_out{n % 2}"]
            pool.dma_start(kvs[0:SEQ, cols].rearrange("(k p) n -> p k n", p=P), kvst[:, n % 2, 0:4, :]).then_inc(out, 16)
            pool.dma_start(kvs[SEQ:TOK, cols], kvst[0:SMP, n % 2, 4, :]).then_inc(out, 16)
        pool.wait_ge(S["kv_out0"], 16 * 6)
        pool.wait_ge(S["kv_out1"], 16 * 6)
        for g in range(3):
            keep = min(WIN[g], SEQ)
            cols = slice(2 * g * AW, 2 * (g + 1) * AW)
            pool.dma_start(O[f"kv{g}_prompt"][0].rearrange("t v h d -> t (v h d)"), kvs[SEQ - keep:SEQ, cols]
                           ).then_inc(S["kv_copy"], 16)
            pool.dma_start(O[f"kv{g}_sample"][:, CACHE[g] - NT:].rearrange("b t v h d -> b t (v h d)"),
                           kvs[SEQ:TOK, cols].rearrange("(b t) n -> b t n", t=NT)).then_inc(S["kv_copy"], 16)
        shift_cache(1, ph="ffn2_in", start=2, every=5)
        squares(4)
        squares(5)
        squares(6)

    @block.scalar
    def _(act):
        me = Steps(act, S["act_self"])

        def split_high(c, s, size):
            if size is None:
                return
            if isinstance(c, int) and c < 2:
                pass
            else:
                act.wait_ge(S["pe_chunk"], c - 1)
            act.wait_ge(w_in[s], (c - s) * 4 + 16)
            nc.scalar.copy(wH[:, s % 2, 0:size], wst[:, s, 0:size]).then_inc(S["w_h"], 1)

        def gain_high(ph, k):
            act.wait_ge(S["x_ready"], KD * XV[ph] + k + 1)
            g = column(k, GAIN[ph])
            if ph == "final":
                nc.scalar.mul(tokens(yg, k), tokens(xT, k), g).then_inc(S["yg_ready"], 1)
            else:
                nc.scalar.mul(tokens(hH, k), tokens(xT, k), g).then_inc(S["h_h"], 1)

        def std(ph):
            act.wait_ge(S["ss_done"], ROUND[ph])
            nc.scalar.activation(rstd[:], pair(1), ACT.Sqrt, scale=1.0 / D, bias=eps[:, 0:1]
                                 ).then_inc(S["std_ready"], 1)

        def std_tokens(ph):
            act.wait_ge(S["ssT_done"], ROUNDT[ph])
            nc.scalar.activation(rstdT[:, 0:4], ps[:, 6, 0:4], ACT.Sqrt, scale=1.0 / D, bias=eps[:, 0:1])
            nc.scalar.activation(rstdT[0:SMP, 4:5], ps[0:SMP, 6, 4:5], ACT.Sqrt, scale=1.0 / D,
                                 bias=eps[0:SMP, 0:1]).then_inc(S["stdT_ready"], 1)

        def ffn_in(ph):
            std(ph)
            n = CHUNKS[ph] // 4

            def body(i, last):
                for u in range(2):
                    f = i * 2 + u
                    size = NEXT_SIZE[ph] if last and u else SIZE[ph]
                    split_high(i * 4 + (CB[ph] + 2 * u + 2), (2 * u + 2) % 4, size)
                    act.wait_ge(S["evac"], i * 4 + (MB[ph] + 2 * u + 5))
                    nc.scalar.activation(ta[:], ta[:], ACT.Silu).then_inc(S["silu_done"], 1)
                    split_high(i * 4 + (CB[ph] + 2 * u + 3), (2 * u + 3) % 4, size)
                    act.wait_ge(S["act_in"], f + (FB[ph] + 1))
                    nc.scalar.copy(tile(actH, f), tb[:]).then_inc(S["act_h"], 1)

            with act.Fori(0, n - 1) as i:
                body(i, False)
            body(n - 1, True)

        def ffn_out(ph):
            def body(i, last):
                c, size = i * 4 + CB[ph], NEXT_SIZE[ph] if last else SIZE[ph]
                split_high(c + 2, 2, SIZE[ph])
                split_high(c + 3, 3, SIZE[ph])
                gain_high(AFTER[ph], i * 2)
                split_high(c + 4, 0, size)
                split_high(c + 5, 1, size)
                gain_high(AFTER[ph], i * 2 + 1)

            with act.Fori(0, 3) as i:
                body(i, False)
            body(3, True)

        split_high(0, 0, SIZE["ffn0_in"])
        split_high(1, 1, SIZE["ffn0_in"])
        act.wait_ge(S["par_ready"], 1)
        for k in range(KD):
            gain_high("ffn0_in", k)
        act.wait_ge(S["b_mm"], 2)
        for n, (a, b) in enumerate(((C1, C2), (C2, C0), (C0, SC))):
            nc.scalar.copy(sbias0[:, a:b], ps[:, 5 + n, 0:b - a]).then_inc(S["b_ev"], 1)
        act.wait_ge(S["rvec_out"], 16)
        act.wait_ge(S["sbd_out"], 16)
        ffn_in("ffn0_in")
        ffn_out("ffn0_out")
        std("pw1")
        nc.scalar.copy(wdH[:], par[:, CD:KD, W_DW:NPAR]).then_inc(S["wd_h"], 1)

        def diagonals(out, w, n, a, b):
            for k in range(a, b):
                nx = nc.scalar.mul(out[n % 2][:, k, :], ident[:], w[:, n, k:k + 1])
            return nx

        def u_high(n):
            act.wait_ge(S["u_ready"], CD + n + 1)
            nc.scalar.copy(uH[n % 2][:], ucat[:, CD + n, 0:30 + SEQ]).then_inc(S["uh_ready"], 1)

        def conv_out(n):
            act.wait_ge(S["conv_mm"], n + 1)
            nc.scalar.activation(tokens(cT, CD + n)[:, 0:SEQ], ps[:, 2 + n, :], ACT.Identity,
                                 bias=par[:, CD + n:CD + n + 1, B_DW]).then_inc(S["cp_ready"], 1)

        high = wdH[:].bitcast(f32)
        for ct in range(KD):
            for v in range(2):
                c = CB["pw1"] + 2 * ct + v + 2
                split_high(c, c % 4, NEXT_SIZE["pw1"] if ct == KD - 1 else SIZE["pw1"])
                if v == 0 and ct < 4:
                    act.wait_ge(S["wd_h"], 1)
                    nx = diagonals(diagH, high, 0, 8 * ct, min(CW, 8 * ct + 8))
                    if ct == 3:
                        nx.then_inc(S["diag_h"], 1)
            act.wait_ge(S["evac"], MB["pw1"] + 2 * ct + 6)
            nc.scalar.activation(tb[:], tb[:], ACT.Sigmoid, bias=column(ct, B_PW1 + 1)).then_inc(S["glu_done"], 1)
            if ct == CD + 1:
                u_high(0)
        act.wait_ge(S["pe_chunk"], CB["pw2"])
        u_high(1)
        diagonals(diagH, high, 1, 0, CW).then_inc(S["diag_h"], 1)
        conv_out(0)
        u_high(2)
        diagonals(diagH, high, 2, 0, CW)
        act.wait_ge(S["wd_ready"], 1)
        diagonals(diagL, wdL, 2, 0, CW).then_inc(S["diag_h"], 1)
        conv_out(1)
        conv_out(2)
        for n in range(4):
            rows = 30 if n < 2 else SMP
            act.wait_ge(S["u_t"], n + 1)
            nc.scalar.copy(cst[0:rows, n // 2, n % 2 * 512:(n % 2 + 1) * 512], ps[0:rows, 4 + n, :]
                           ).then_inc(S["u_ev"], 1)
        for k in range(KD):
            act.wait_ge(S["cc_ready"], k + 1)
            if k >= 2:
                act.wait_ge(S["var_mm"], k - 1)
            nc.scalar.activation((ta, tb)[k % 2][:], cT[:, k], ACT.Square).then_inc(S["csq_ready"], 1)
        act.wait_ge(S["var_mm"], KD)
        nc.scalar.activation(rstd[:], pair(1), ACT.Sqrt, scale=1.0 / D, bias=eps[:, 0:1]
                             ).then_inc(S["lnstd_ready"], 1)
        for k in range(KD):
            act.wait_ge(S["ln_in"], k + 1)
            me.mark(nc.scalar.activation(cT[:, k], cT[:, k], ACT.Silu, scale=par[:, k:k + 1, LN_G],
                                         bias=par[:, k:k + 1, LN_B]))
            me.wait()
            nc.scalar.copy(cH[:, k], cT[:, k]).then_inc(S["h_h"], 1)
        for m in range(KD):
            c = CB["pw2"] + m + 2
            split_high(c, c % 4, SIZE["pw2"] if m < KD - 2 else NEXT_SIZE["pw2"])
            gain_high("ffn1_in", m)
        act.wait_ge(S["conv_out"], 16 * 9)
        ffn_in("ffn1_in")
        ffn_out("ffn1_out")
        std_tokens("kv")
        with act.Fori(0, 5) as i:
            for s in range(4):
                split_high(i * 4 + (CB["kv"] + 2 + s), (s + 2) % 4, SIZE["kv"])
        for s in range(4):
            split_high(CB["kv"] + 20 + 2 + s, (s + 2) % 4, SIZE["kv"] if s < 2 else NEXT_SIZE["kv"])
        act.wait_ge(S["pe_chunk"], CB["ffn2_in"])
        for k in range(KD):
            gain_high("ffn2_in", k)
        act.wait_ge(S["kv_out0"], 16 * 6)
        act.wait_ge(S["kv_out1"], 16 * 6)
        ffn_in("ffn2_in")
        ffn_out("ffn2_out")
        std("q")
        for c in range(12):
            split_high(CB["q"] + c + 2, (c + 2) % 4, SIZE["q"] if c < 10 else NEXT_SIZE["q"])
        with act.Fori(0, PAIRS) as j:
            act.wait_ge(S["kt_tr"], j + 1)
            nc.scalar.copy(kT[:, 2, :], ps[:, 2, :]).then_inc(S["kt_a"], 1)

            def exp(u):
                act.wait_ge(S["sm_ready"], j * 8 + (u + 1))
                o = u % 2
                nc.scalar.activation(sP[:, o, :], sP[:, o, :], ACT.Exp, bias=stat[:, u:u + 1],
                                     accum_out=stat[:, 8 + u:9 + u]).then_inc(S["p_ready"], 1)

            exp(0)
            exp(1)
            for u in range(8):
                act.wait_ge(S["pt_done"], j * 8 + (u + 1))
                if u >= 2:
                    act.wait_ge(S["pv_done"], j * 8 + (u - 1))
                nc.scalar.copy(pT[:, u % 2, :], ps[:, 4:6, :].rearrange("p a b -> p (a b)")[:, 0:768]
                               ).then_inc(S["pt_ready"], 1)
                if u < 6:
                    exp(u + 2)
        def kt_copies(b):
            for g in range(1, 12, 2):
                act.wait_ge(S["ktr"], b * 12 + (g + 1))
                jj, x = divmod(g, 3)
                a, n = ((C1, 512), (C2, 512), (C0, SC - C0))[x]
                nc.scalar.copy(kTs[:, jj, a:a + n], ps[:, (3, 4, 5, 7)[g % 4], 0:n]).then_inc(S["kta"], 1)

        def sample_body(b, last):
            act.wait_ge(S["sm2"], b + 1)
            nc.scalar.activation(sS[:], sS[:], ACT.Exp, bias=stS[:, 0:1], accum_out=stS[:, 1:2]).then_inc(S["p2"], 1)
            if not last:
                kt_copies(b + 1)
            for x in range(2):
                act.wait_ge(S["ptr_mm"], b * 3 + (x + 1))
                nc.scalar.copy(ptS[:, 4 * x:4 * x + 4, :].rearrange("p a b -> p (a b)"), ps[:, 3 + x, :]
                               ).then_inc(S["ptr_a"], 1)

        kt_copies(0)
        with act.Fori(0, NB - 1) as b:
            sample_body(b, False)
        sample_body(NB - 1, True)
        act.wait_ge(S["o2"], NB)
        for k in range(PAIRS):
            nc.scalar.copy(oH[:, k], oT[:, k]).then_inc(S["h_h"], 1)
        for m in range(KD):
            if m % 2 == 0:
                c = m // 2 + 2
                split_high(CB["wo"] + c, c % 4, SIZE["wo"] if c < 4 else NEXT_SIZE["wo"])
            gain_high("ffn3_in", m)
        ffn_in("ffn3_in")
        ffn_out("ffn3_out")
        std_tokens("final")

    @block.vector
    def _(dve):
        me = Steps(dve, S["dve_self"])

        def split_low(c, s, size):
            if size is None:
                return
            dve.wait_ge(S["w_h"], c + 1)
            nc.vector.tensor_tensor(wL[:, s % 2, 0:size], wst[:, s, 0:size], wH[:, s % 2, 0:size].bitcast(f32),
                                    ALU.subtract).then_inc(S["w_ready"], 1)

        def gain_low(ph, k):
            if ph == "final":
                return
            dve.wait_ge(S["h_h"], k + (HB[ph] + 1))
            nc.vector.scalar_tensor_tensor(tile(hL, k), tile(xT, k), column(k, GAIN[ph]), tile(hH, k).bitcast(f32),
                                           ALU.mult, ALU.subtract).then_inc(S["h_ready"], 1)

        def low_of(ph, low, src, high, k):
            dve.wait_ge(S["h_h"], HB[ph] + k + 1)
            nc.vector.tensor_tensor(low[:, k], src[:, k], high[:, k].bitcast(f32), ALU.subtract
                                    ).then_inc(S["h_ready"], 1)

        def invert_std(ph):
            dve.wait_ge(S["std_ready"], ROUND[ph])
            me.mark(nc.vector.reciprocal(rstd[:], rstd[:]))
            me.wait()

        def ffn_in(ph):
            invert_std(ph)
            n = CHUNKS[ph] // 4
            mb, cb, fb = MB[ph], CB[ph], FB[ph]

            def body(i, last):
                for u in range(2):
                    f = i * 2 + u
                    size = NEXT_SIZE[ph] if last and u else SIZE[ph]
                    for v in range(2):
                        s = 2 * u + v
                        split_low(i * 4 + (cb + s + 2), (s + 2) % 4, size)
                        dve.wait_ge(S["pe_chunk"], i * 4 + (cb + s + 1))
                        nc.vector.tensor_tensor((ta, tb)[v][:], pair((2 + s) % 4), rstd[:], ALU.mult
                                                ).then_inc(S["evac"], 1)
                    dve.wait_ge(S["evac"], i * 4 + (mb + 2 * u + 6))
                    dve.wait_ge(S["silu_done"], f + (fb + 1))
                    nc.vector.tensor_tensor(tb[:], ta[:], tb[:], ALU.mult).then_inc(S["act_in"], 1)
                    dve.wait_ge(S["act_h"], f + (fb + 1))
                    nc.vector.tensor_tensor(tile(actL, f), tb[:], tile(actH, f).bitcast(f32), ALU.subtract
                                            ).then_inc(S["act_ready"], 1)

            with dve.Fori(0, n - 1) as i:
                body(i, False)
            body(n - 1, True)

        def residual(ph, m, chunk, p, scale):
            if ph == "wo" and m % 2 == 0:
                dve.wait_ge(S["wo_even"], m // 2 + 1)
            else:
                dve.wait_ge(S["pe_chunk"], chunk + 1)
            if ph == "pw2":
                nx = nc.vector.scalar_tensor_tensor(tile(xT, m), pair(p), column(m, B_PW2), tile(xT, m),
                                                    ALU.add, ALU.add)
            else:
                nx = nc.vector.scalar_tensor_tensor(tile(xT, m), pair(p), scale, tile(xT, m), ALU.mult, ALU.add)
            nx.then_inc(S["x_ready"], 1)

        def ffn_out(ph):
            def body(i, last):
                c, size = i * 4 + CB[ph], NEXT_SIZE[ph] if last else SIZE[ph]
                split_low(c + 2, 2, SIZE[ph])
                residual(ph, i * 2, c + 1, 0, 0.5)
                split_low(c + 3, 3, SIZE[ph])
                split_low(c + 4, 0, size)
                gain_low(AFTER[ph], i * 2)
                residual(ph, i * 2 + 1, c + 3, 1, 0.5)
                split_low(c + 5, 1, size)
                gain_low(AFTER[ph], i * 2 + 1)

            with dve.Fori(0, 3) as i:
                body(i, False)
            body(3, True)

        nc.vector.memset(ones[:], 1.0)
        nc.vector.memset(relE[32:33, :], NEG)
        me.mark(nc.vector.memset(sel[:], 0.0))
        nc.vector.memset(eps[:], EPS).then_inc(S["consts_ready"], 1)
        dve.wait_ge(S["par_t"], 1)
        nc.vector.tensor_copy(par[:], ps[:, 0, 0:KD * NPAR].rearrange("p (k n) -> p k n", k=KD)
                              ).then_inc(S["par_ready"], 1)
        for k in range(KD):
            dve.wait_ge(S["x_t"], k + 1)
            o, p = tokens(xT, k), 1 + k % 2
            nc.vector.tensor_copy(o[:, 0:SEQ], ps[:, 2 * p, 0:SEQ])
            nc.vector.tensor_copy(o[:, SEQ:TOK], ps[:, 2 * p + 1, 0:SMP]).then_inc(S["x_ready"], 1)
        split_low(0, 0, SIZE["ffn0_in"])
        split_low(1, 1, SIZE["ffn0_in"])
        dve.wait_ge(S["par_ready"], 1)
        dve.wait_ge(S["x_ready"], KD)
        for k in range(KD):
            gain_low("ffn0_in", k)
        nc.vector.memset(void[:], 0.0).then_inc(S["evac"], 4)
        me.wait()
        dve.wait_ge(S["bias_in"], 16 * 9)
        for tg in range(2):
            for t4 in range(4):
                t = 4 * tg + t4
                q = slice(32 * t4, 32 * t4 + 32)
                dst = sel[q, tg, :, :].rearrange("p g (j x) -> p g j x", j=PAIRS)[:, :, :, t:t + NT + 1:NT]
                src = relq[q, :].rearrange("p (g j x) -> p g j x", g=3, j=PAIRS)
                nx = nc.vector.tensor_copy(dst.rearrange("p g j x -> p (g j) x"), src.rearrange("p g j x -> p (g j) x"))
        nx.then_inc(S["sel_ready"], 1)
        dve.wait_ge(S["b_mm"], 1)
        for n in range(3):
            a, b = n * 512, min(R_LEN, (n + 1) * 512)
            nc.vector.tensor_copy(Rsb[:, a:b], ps[0:24, 2 + n, 0:b - a]).then_inc(S["b_ev"], 1)
        ffn_in("ffn0_in")
        ffn_out("ffn0_out")

        invert_std("pw1")
        me.mark(nc.vector.memset(ucat[:, :, 0:30], 0.0))
        us = ucat[:, :, 30 + SEQ:UW].rearrange("p k (b t) -> p k b t", b=NB)
        for k in range(KD):
            dve.wait_ge(S["st_t"], k + 1)
            for h in range(2):
                nx = nc.vector.tensor_copy(us[:, k, 4 * h:4 * h + 4, 0:30],
                                           ps[:, 6 + k % 2, h * 120:h * 120 + 120].rearrange("p (b t) -> p b t", b=4))
            nx.then_inc(S["st_ready"], 1)

        done = [0]

        def taps(n):
            for x in range(done[0], min(done[0] + n, CD * CW)):
                ct, k = divmod(x, CW)
                c, w, u = tokens(cT, ct)[:, 0:SEQ], column(ct, W_DW + k), ucat[:, ct, k:k + SEQ]
                if k == 0:
                    dve.wait_ge(S["u_ready"], ct + 1)
                    nx = nc.vector.tensor_scalar(c, u, w, column(ct, B_DW), ALU.mult, ALU.add)
                else:
                    me.wait()
                    nx = nc.vector.scalar_tensor_tensor(c, u, w, c, ALU.mult, ALU.add)
                if k < CW - 1:
                    me.mark(nx)
                else:
                    nx.then_inc(S["c_ready"], 1)
            done[0] += n

        dve.wait_ge(S["wd_h"], 1)
        nc.vector.tensor_tensor(wdL[:], par[:, CD:KD, W_DW:NPAR], wdH[:].bitcast(f32), ALU.subtract
                                ).then_inc(S["wd_ready"], 1)
        for ct in range(KD):
            size = NEXT_SIZE["pw1"] if ct == KD - 1 else SIZE["pw1"]
            for v in range(2):
                c = CB["pw1"] + 2 * ct + v
                split_low(c + 2, (c + 2) % 4, size)
                dve.wait_ge(S["pe_chunk"], c + 1)
                if ct and v == 0:
                    dve.wait_ge(S["u_ready"], ct)
                nc.vector.tensor_tensor((ta, tb)[v][:], pair((2 + 2 * ct + v) % 4), rstd[:], ALU.mult
                                        ).then_inc(S["evac"], 1)
                if ct:
                    taps(4 + v)
            dve.wait_ge(S["evac"], MB["pw1"] + 2 * ct + 6)
            dve.wait_ge(S["glu_done"], ct + 1)
            a, g, w = tokens(ta), tokens(tb), column(ct, B_PW1)
            nc.vector.scalar_tensor_tensor(ucat[:, ct, 30:30 + SEQ], a[:, 0:SEQ], w, g[:, 0:SEQ], ALU.add, ALU.mult)
            nc.vector.scalar_tensor_tensor(
                us[:, ct, :, 30:30 + NT], a[:, SEQ:TOK].rearrange("p (b t) -> p b t", b=NB), w,
                g[:, SEQ:TOK].rearrange("p (b t) -> p b t", b=NB), ALU.add, ALU.mult).then_inc(S["u_ready"], 1)
        dve.wait_ge(S["u_ready"], KD)
        nc.vector.tensor_copy(un[:].rearrange("p k (b t) -> p k b t", b=NB), us[:, :, :, 30:30 + NT]
                              ).then_inc(S["un_ready"], 1)
        taps(3 * CW - done[0])
        dve.wait_ge(S["uh_ready"], 3)
        nc.vector.tensor_tensor(uL[0][:], ucat[:, CD + 2, 0:30 + SEQ], uH[0][:].bitcast(f32), ALU.subtract
                                ).then_inc(S["ul7_ready"], 1)
        taps(CD * CW - done[0])
        dve.wait_ge(S["c_ready"], CD)
        dve.wait_ge(S["mu_mm"], KD)
        for k in range(KD):
            nc.vector.scalar_tensor_tensor(cT[:, k], pair(0), -1.0 / D, cT[:, k], ALU.mult, ALU.add
                                           ).then_inc(S["cc_ready"], 1)
        dve.wait_ge(S["lnstd_ready"], 1)
        me.mark(nc.vector.reciprocal(rstd[:], rstd[:]))
        me.wait()
        dve.wait_ge(S["cc_ready"], KD)
        for k in range(KD):
            nc.vector.tensor_tensor(cT[:, k], cT[:, k], rstd[:], ALU.mult).then_inc(S["ln_in"], 1)
            if k:
                low_of("pw2", cL, cT, cH, k - 1)
        low_of("pw2", cL, cT, cH, KD - 1)
        for m in range(KD):
            c = CB["pw2"] + m
            residual("pw2", m, c, m % 2, None)
            split_low(c + 2, (m + 2) % 4, SIZE["pw2"] if m < KD - 2 else NEXT_SIZE["pw2"])
            gain_low("ffn1_in", m)
        ffn_in("ffn1_in")
        ffn_out("ffn1_out")

        dve.wait_ge(S["stdT_ready"], 1)
        me.mark(nc.vector.reciprocal(rstdT[:, 0:4], rstdT[:, 0:4]))
        nc.vector.reciprocal(rstdT[0:SMP, 4:5], rstdT[0:SMP, 4:5]).then_inc(S["kv_evac"], 5)
        me.wait()
        dve.wait_ge(S["kv_evac"], 5)
        for n in range(6):
            for s in range(4):
                c = 4 * n + s + 2
                if s == 3:
                    if n >= 2:
                        dve.wait_ge(S[f"kv_out{n % 2}"], 32 * (n // 2))
                    dve.wait_ge(S["pe_chunk"], CB["kv"] + 4 * n + 4)
                    for t in range(TT):
                        r = P if t < 4 else SMP
                        nc.vector.tensor_scalar(kvst[0:r, n % 2, t, :], ps[0:r, t, :], rstdT[0:r, t:t + 1], None,
                                                ALU.mult).then_inc(S["kv_evac"], 1)
                split_low(CB["kv"] + c, c % 4, SIZE["kv"] if c < 24 else NEXT_SIZE["kv"])
        for k in range(KD):
            gain_low("ffn2_in", k)
        ffn_in("ffn2_in")
        ffn_out("ffn2_out")

        invert_std("q")
        for c in range(12):
            split_low(CB["q"] + c + 2, (c + 2) % 4, SIZE["q"] if c < 10 else NEXT_SIZE["q"])
            dve.wait_ge(S["pe_chunk"], CB["q"] + c + 1)
            nc.vector.tensor_tensor(qT[:, c, :].rearrange("p (a b) -> p a b", a=2), pair((2 + c) % 4), rstd[:],
                                    ALU.mult).then_inc(S["evac"], 1)
        dve.wait_ge(S["evac"], MB["q"] + 12 + 4)

        nc.vector.memset(void[:], 0.0).then_inc(S["s_evac"], 1)
        qp = qT[:, :, 0:SEQ].rearrange("p (g j) (a r) -> p g j r a", g=3, r=4)

        def bias_max(j, u):
            r, h2, o = u // 2, u % 2, u % 2
            if u >= 2:
                dve.wait_ge(S["pt_done"], j * 8 + (u - 1))
            dve.wait_ge(S["s_done"], j * 8 + (u + 1))
            nc.vector.scalar_tensor_tensor(sP[:, o, 0:SEQ], ps[:, 2 * o, :], HD ** -0.5,
                                           bT[:, h2, 3 - r:3 - r + SEQ], ALU.mult, ALU.add)
            nc.vector.scalar_tensor_tensor(sP[:, o, SEQ:768], ps[:, 2 * o + 1, 0:256], HD ** -0.5,
                                           bT[:, h2, T0W:], ALU.mult, ALU.add).then_inc(S["s_evac"], 1)
            dve.wait_ge(S["s_evac"], j * 8 + (u + 2))
            me.mark(nc.vector.reduce_max(stat[:, 16 + u:17 + u], sP[:, o, :], AX.X))
            me.wait()
            nc.vector.tensor_scalar(stat[:, u:u + 1], stat[:, 16 + u:17 + u], -1.0, None, ALU.mult
                                    ).then_inc(S["sm_ready"], 1)

        with dve.Fori(0, PAIRS) as j:
            me.loop(j, 16)
            for g in range(3):
                src = qp[:, g, bass.ds(j, 1)].rearrange("p o r a -> p (o r) a")
                nx = nc.vector.tensor_copy(qc[:, g, :, ::-1], src)
            nx.then_inc(S["qc_ready"], 1)
            dve.wait_ge(S["kt_tr"], j + 1)
            for g in range(2):
                nx = nc.vector.tensor_copy(kT[:, g, :], ps[:, g, :])
            nx.then_inc(S["kt_d"], 1)
            dve.wait_ge(S["b_in"], j * 96 + 96)
            bias_max(j, 0)
            bias_max(j, 1)
            for u in range(8):
                if u < 6:
                    bias_max(j, u + 2)
                o = u % 2
                dve.wait_ge(S["pv_done"], j * 8 + (u + 1))
                me.mark(nc.vector.reciprocal(stat[:, 24 + u:25 + u], stat[:, 8 + u:9 + u]))
                me.wait()
                nc.vector.tensor_scalar(oS[:, u // 2, HD * o:HD * (o + 1)], ps[:, 6 + o, 0:HD],
                                        stat[:, 24 + u:25 + u], None, ALU.mult).then_inc(S["o_evac"], 1)
            dve.wait_ge(S["ot_done"], j + 1)
            ot = tokens(oT, j)[:, 0:SEQ].rearrange("p (a r) -> p r a", r=4)
            nc.vector.tensor_copy(ot, ps[:, 4, :].rearrange("p (r a) -> p r a", r=4)[:, :, ::-1]
                                  ).then_inc(S["ot_ready"], 1)
            me.end(PAIRS)

        me.mark(nc.vector.memset(qs[:], 0.0))

        oTf = oT[:].rearrange("p j a b -> p j (a b)")

        def queries(b):
            for h2 in range(2):
                q = slice(HD * h2, HD * (h2 + 1))
                col = (SEQ + NT * b) if isinstance(b, int) else b * NT + SEQ
                nx = nc.vector.tensor_copy(qs[q, :, NT * h2:NT * (h2 + 1)], qT[q, :, bass.ds(col, NT)])
            nx.then_inc(S["q_ready"], 1)

        def kt_copies(b):
            for g in range(0, 12, 2):
                dve.wait_ge(S["ktr"], b * 12 + (g + 1))
                jj, x = divmod(g, 3)
                a, n = ((C1, 512), (C2, 512), (C0, SC - C0))[x]
                nc.vector.tensor_copy(kTs[:, jj, a:a + n], ps[:, (3, 4, 5, 7)[g % 4], 0:n]).then_inc(S["ktd"], 1)

        def sample_body(b, last):
            dve.wait_ge(S["ss_mm"], b + 1)
            nc.vector.scalar_tensor_tensor(sS[:, 0:C0], ps[:, 0:2, :].rearrange("p a b -> p (a b)"), HD ** -0.5,
                                           sbias[:, 0:C0], ALU.mult, ALU.add)
            me.mark(nc.vector.scalar_tensor_tensor(sS[:, C0:SC], ps[:, 2, 0:SC - C0], HD ** -0.5, sbias[:, C0:SC],
                                                   ALU.mult, ALU.add))
            me.wait()
            me.mark(nc.vector.reduce_max(stS[:, 2:3], sS[:], AX.X))
            me.wait()
            nc.vector.tensor_scalar(stS[:, 0:1], stS[:, 2:3], -1.0, None, ALU.mult).then_inc(S["sm2"], 1)
            if not last:
                queries(b + 1)
            dve.wait_ge(S["p2"], b + 1)
            me.mark(nc.vector.reciprocal(stS[:, 3:4], stS[:, 1:2]))
            me.wait()
            nc.vector.tensor_scalar(sS[:], sS[:], stS[:, 3:4], None, ALU.mult).then_inc(S["pn"], 1)
            if not last:
                kt_copies(b + 1)
            dve.wait_ge(S["ptr_mm"], b * 3 + 3)
            nc.vector.tensor_copy(ptS[:, 8, :], ps[:, 5, 0:P])
            nc.vector.tensor_copy(ptS[0:24, 9, :], ps[0:24, 5, P:2 * P]).then_inc(S["ptr_d"], 1)
            dve.wait_ge(S["pv2"], b + 1)
            for h2 in range(2):
                q = slice(HD * h2, HD * (h2 + 1))
                col = (SEQ + NT * b) if isinstance(b, int) else b * NT + SEQ
                o = oTf[q, :, bass.ds(col, NT)]
                nx = nc.vector.tensor_copy(o, ps[q, 6, 0:P].rearrange("p (j x) -> p j x", j=PAIRS)[:, :, NT * h2:NT * (h2 + 1)])
            nx.then_inc(S["o2"], 1)

        dve.wait_ge(S["sbias_in"], 16)
        me.wait()
        queries(0)
        kt_copies(0)
        with dve.Fori(0, NB - 1) as b:
            me.loop(b, 3)
            sample_body(b, False)
            me.end(NB - 1)
        sample_body(NB - 1, True)
        dve.wait_ge(S["o2"], NB)
        for k in range(PAIRS):
            low_of("wo", oL, oT, oH, k)
        for m in range(KD):
            residual("wo", m, CB["wo"] + m // 2, m % 2, 1.0)
            if m % 2 == 1:
                c = m // 2 + 2
                split_low(CB["wo"] + c, c % 4, SIZE["wo"] if c < 4 else NEXT_SIZE["wo"])
            gain_low("ffn3_in", m)
        ffn_in("ffn3_in")
        ffn_out("ffn3_out")

        dve.wait_ge(S["stdT_ready"], 2)
        me.mark(nc.vector.reciprocal(rstdT[:, 0:4], rstdT[:, 0:4]))
        me.mark(nc.vector.reciprocal(rstdT[0:SMP, 4:5], rstdT[0:SMP, 4:5]))
        me.wait()
        me.wait(1)
        for t in range(TT):
            r = P if t < 4 else SMP
            dve.wait_ge(S["yt"], t + 1)
            if t >= 2:
                dve.wait_ge(S["y_out"], 16 * (t - 1))
            nc.vector.tensor_scalar(yst[0:r, t % 2, :], ps[0:r, 2 * (t % 2):2 * (t % 2) + 2, :].rearrange(
                "p a b -> p (a b)"), rstdT[0:r, t:t + 1], None, ALU.mult).then_inc(S["y_ready"], 1)

    @block.tensor
    def _(pe):
        def split_mm(outs, wh, wl, xh, xl, start, stop):
            for a, b, first in ((wh, xh, True), (wh, xl, False), (wl, xh, False)):
                for t in range(2):
                    nx = nc.tensor.matmul(outs[t], a, b[:, t, :], start=start and first,
                                          stop=stop and b is xh and not first)
            return nx

        def halves(p):
            return [ps[:, 2 * p + t, 0:HALF] for t in range(2)]

        def square_sum():
            for t in range(2):
                nx = nc.tensor.matmul(ps[:, 2 + t, 0:HALF], ones[:], tb[:, t, :], start=True, stop=True)
            return nx

        def square_sum_tokens():
            t_ = tokens(tb)
            for t in range(TT):
                r = P if t < 4 else SMP
                nx = nc.tensor.matmul(ps[0:r, 6, t:t + 1], t_[:, t * P:t * P + r], ones[:, 0:1], start=True, stop=True)
            nx.then_inc(S["ssT_done"], 1)

        def in_phase(ph, squared=False):
            n, cb, mb = CHUNKS[ph] // 4, CB[ph], MB[ph]

            def body(i, first):
                for s in range(4):
                    pe.wait_ge(S["w_ready"], i * 4 + (cb + s + 1))
                    pe.wait_ge(S["evac"], i * 4 + (mb + s + 1))
                    if first and s == 3:
                        pe.wait_ge(S["std_ready"], ROUND[ph])
                    for k in range(KD):
                        if first and s == 0:
                            pe.wait_ge(S["h_ready"], HB[ph] + k + 1)
                        nx = split_mm(halves((2 + s) % 4), wH[:, s % 2, k * P:(k + 1) * P],
                                      wL[:, s % 2, k * P:(k + 1) * P], hH[:, k], hL[:, k], k == 0, k == KD - 1)
                    nx.then_inc(S["pe_chunk"], 1)
                    if first and s == 0 and not squared:
                        pe.wait_ge(S["sq_ready"], XV[ph] + 1)
                        square_sum().then_inc(S["ss_done"], 1)

            body(0, True)
            if n > 1:
                with pe.Fori(1, n) as i:
                    body(i, False)

        def out_phase(ph, fph):
            def body(i):
                for s in range(4):
                    u, v = divmod(s, 2)
                    pe.wait_ge(S["w_ready"], i * 4 + (CB[ph] + s + 1))
                    if v == 0:
                        pe.wait_ge(S["evac"], MB[ph] + 3 + u)
                        pe.wait_ge(S["x_ready"], i * 2 + (KD * XV[AFTER[ph]] + u - 1))
                    for k in range(KF // 2):
                        kf = v * (KF // 2) + k
                        if kf in (0, KF - 2, KF - 1):
                            pe.wait_ge(S["act_ready"], FB[fph] + (KF - 2 if kf == 0 else kf + 1))
                        nx = split_mm(halves(u), wH[:, s % 2, k * P:(k + 1) * P], wL[:, s % 2, k * P:(k + 1) * P],
                                      actH[:, kf], actL[:, kf], kf == 0, kf == KF - 1)
                    nx.then_inc(S["pe_chunk"], 1)

            with pe.Fori(0, 4) as i:
                body(i)

        pe.wait_ge(S["ident_ready"], 1)
        pe.wait_ge(S["consts_ready"], 1)
        pe.wait_ge(S["par_in"], 16 * 9)
        for k in range(KD):
            nx = nc.tensor.transpose(ps[:, 0, k * NPAR:(k + 1) * NPAR], parR[:, k * P:(k + 1) * P],
                                     ident[0:NPAR, 0:NPAR])
        nx.then_inc(S["par_t"], 1)
        pe.wait_ge(S["x_in"], 32)
        for k in range(KD):
            p = 1 + k % 2
            if k >= 2:
                pe.wait_ge(S["x_ready"], k - 1)
            for t in range(4):
                nc.tensor.transpose(ps[:, 2 * p, t * P:(t + 1) * P], xr[:, t, k * P:(k + 1) * P], ident[:])
            nc.tensor.transpose(ps[:, 2 * p + 1, 0:SMP], xr[0:SMP, 4, k * P:(k + 1) * P], ident[0:SMP, 0:SMP]
                                ).then_inc(S["x_t"], 1)
        pe.wait_ge(S["bias_in"], 16 * 9)
        pe.wait_ge(S["sel_ready"], 1)
        for n in range(3):
            a, b = n * 512, min(R_LEN, (n + 1) * 512)
            nx = nc.tensor.matmul(ps[0:24, 2 + n, 0:b - a], relE[:], E1[:, a:b], start=True, stop=True)
        nx.then_inc(S["b_mm"], 1)
        def sample_bias(out, a, b, g, step=1):
            for tg in range(2):
                nc.tensor.matmul(out, sel[:, tg, g, :], E2[:, tg, a:b:step], start=tg == 0, stop=False)
            return nc.tensor.matmul(out, selm[:], Ebad[:, a:b:step], start=False, stop=True)
        sample_bias(ps[:, 5, :], C1, C2, 1)
        sample_bias(ps[:, 6, :], C2, C0, 2)
        sample_bias(ps[:, 7, 0:P], C0, CN, 0)
        for g in range(3):
            nx = sample_bias(ps[:, 7, P + g:SC - C0:3], CN + g, SC, g, 3)
        nx.then_inc(S["b_mm"], 1)
        pe.wait_ge(S["b_ev"], 6)

        in_phase("ffn0_in")
        out_phase("ffn0_out", "ffn0_in")

        pe.wait_ge(S["st_in"], 16)
        for k in range(KD):
            if k >= 2:
                pe.wait_ge(S["st_ready"], k - 1)
            for h in range(2):
                nx = nc.tensor.transpose(ps[:, 6 + k % 2, h * 120:(h + 1) * 120], stR[:, h, k * P:(k + 1) * P],
                                         ident[0:120, 0:120])
            nx.then_inc(S["st_t"], 1)
            if k == 0:
                pe.wait_ge(S["sq_ready"], XV["pw1"] + 1)
                square_sum().then_inc(S["ss_done"], 1)
        pe.wait_ge(S["st_ready"], KD)
        in_phase("pw1", squared=True)
        pe.wait_ge(S["evac"], MB["pw1"] + 16 + 4)

        def convolve(n):
            o = n % 2
            pe.wait_ge(S["uh_ready"], n + 1)
            pe.wait_ge(S["diag_h"], n + 1)
            if n < 2:
                pe.wait_ge(S["diag_l"], n + 1)
                pe.wait_ge(S["ul_ready"], n + 1)
            else:
                pe.wait_ge(S["ul7_ready"], 1)
            for k in range(CW):
                h, l, x, y = diagH[o][:, k, :], diagL[o][:, k, :], uH[o][:, k:k + SEQ], uL[o][:, k:k + SEQ]
                nc.tensor.matmul(ps[:, 2 + n, :], h, x, start=k == 0, stop=False)
                nc.tensor.matmul(ps[:, 2 + n, :], h, y, start=False, stop=False)
                nx = nc.tensor.matmul(ps[:, 2 + n, :], l, x, start=False, stop=k == CW - 1)
            nx.then_inc(S["conv_mm"], 1)

        def mean_of(k, last=False):
            if k < CD:
                pe.wait_ge(S["c_ready"], k + 1)
            else:
                pe.wait_ge(S["cp_ready"], k - CD + 1)
            pe.wait_ge(S["cs_ready"], k // 4 + 1)
            for t in range(2):
                nx = nc.tensor.matmul(ps[:, t, 0:HALF], ones[:], cT[:, k, t, :], start=k == 0, stop=last)
            nx.then_inc(S["mu_mm"], 1)

        convolve(0)
        mean_of(0)
        mean_of(1)
        convolve(1)
        convolve(2)
        mean_of(2)
        pe.wait_ge(S["un_ready"], 1)
        pe.wait_ge(S["cp_ready"], CP)
        for n in range(4):
            for k in range(4):
                kk = n % 2 * 4 + k
                if n < 2:
                    nx = nc.tensor.transpose(ps[0:30, 4 + n, k * P:(k + 1) * P], ucat[:, kk, SEQ:SEQ + 30], ident[:])
                else:
                    nx = nc.tensor.transpose(ps[0:SMP, 4 + n, k * P:(k + 1) * P], un[:, kk], ident[:])
            nx.then_inc(S["u_t"], 1)
        mean_of(3)
        for k in range(CD, KD):
            mean_of(k)
        mean_of(CD - 1, last=True)
        for k in range(KD):
            pe.wait_ge(S["csq_ready"], k + 1)
            for t in range(2):
                nx = nc.tensor.matmul(ps[:, 2 + t, 0:HALF], ones[:], (ta, tb)[k % 2][:, t, :], start=k == 0,
                                      stop=k == KD - 1)
            nx.then_inc(S["var_mm"], 1)
        for m in range(KD):
            pe.wait_ge(S["w_ready"], CB["pw2"] + m + 1)
            if m >= 2:
                pe.wait_ge(S["x_ready"], KD * 2 + m - 1)
            if m == 1:
                pe.wait_ge(S["lnstd_ready"], 1)
            for k in range(KD):
                if m == 0:
                    pe.wait_ge(S["h_ready"], HB["pw2"] + k + 1)
                nx = split_mm(halves(m % 2), wH[:, m % 2, k * P:(k + 1) * P], wL[:, m % 2, k * P:(k + 1) * P],
                              cH[:, k], cL[:, k], k == 0, k == KD - 1)
            nx.then_inc(S["pe_chunk"], 1)

        in_phase("ffn1_in")
        out_phase("ffn1_out", "ffn1_in")

        pe.wait_ge(S["sq_ready"], XV["kv"] + 1)
        square_sum_tokens()
        for k in range(KD):
            pe.wait_ge(S["h_ready"], HB["kv"] + k + 1)
        hHf, hLf = hH[:].rearrange("p k a b -> p k (a b)"), hL[:].rearrange("p k a b -> p k (a b)")
        with pe.Fori(0, 6) as n:
            for s in range(4):
                pe.wait_ge(S["w_ready"], n * 4 + (CB["kv"] + s + 1))
                for t in range(TT):
                    r = P if t < 4 else SMP
                    if s == 0:
                        pe.wait_ge(S["kv_evac"], n * 5 + (t + 1))
                    for k2 in range(2):
                        k = 2 * s + k2
                        xh, xl = hHf[:, k, t * P:t * P + r], hLf[:, k, t * P:t * P + r]
                        a, b = wH[:, s % 2, k2 * AW:(k2 + 1) * AW], wL[:, s % 2, k2 * AW:(k2 + 1) * AW]
                        nc.tensor.matmul(ps[0:r, t, :], xh, a, start=k == 0, stop=False)
                        nc.tensor.matmul(ps[0:r, t, :], xh, b, start=False, stop=False)
                        nx = nc.tensor.matmul(ps[0:r, t, :], xl, a, start=False, stop=k == KD - 1)
                nx.then_inc(S["pe_chunk"], 1)
        pe.wait_ge(S["kv_evac"], 35)

        in_phase("ffn2_in")
        out_phase("ffn2_out", "ffn2_in")

        in_phase("q")

        pe.wait_ge(S["evac"], MB["q"] + 12 + 4)
        with pe.Fori(0, PAIRS) as j:
            pe.wait_ge(S["k_in"], j * 48 + 48)
            pe.wait_ge(S["s_evac"], j * 8 + 1)
            for x in range(12):
                nx = nc.tensor.transpose(ps[:, x // 4, x % 4 * P:(x % 4 + 1) * P], kin[:, x, :], ident[:])
            nx.then_inc(S["kt_tr"], 1)
            pe.wait_ge(S["qc_ready"], j + 1)
            pe.wait_ge(S["kt_d"], j + 1)
            pe.wait_ge(S["kt_a"], j + 1)

            def scores(u):
                r, h2, o = u // 2, u % 2, u % 2
                q = slice(HD * h2, HD * (h2 + 1))
                if u >= 2:
                    pe.wait_ge(S["s_evac"], j * 8 + u)
                nc.tensor.matmul(ps[:, 2 * o, :], qc[q, 0, r, :], kT[q, 0, :], start=True, stop=True)
                for g in (1, 2):
                    nx = nc.tensor.matmul(ps[:, 2 * o + 1, (g - 1) * P:g * P], qc[q, g, r, :],
                                          kT[q, g, r * P:(r + 1) * P], start=True, stop=True)
                nx.then_inc(S["s_done"], 1)

            scores(0)
            scores(1)
            pe.wait_ge(S["v_in"], j * 48 + 48)
            for u in range(8):
                r, h2, o = u // 2, u % 2, u % 2
                pe.wait_ge(S["p_ready"], j * 8 + (u + 1))
                for x in range(6):
                    nx = nc.tensor.transpose(ps[:, 4 + x // 4, x % 4 * P:(x % 4 + 1) * P],
                                             sP[:, o, x * P:(x + 1) * P], ident[:])
                nx.then_inc(S["pt_done"], 1)
                if u < 6:
                    scores(u + 2)
                pe.wait_ge(S["pt_ready"], j * 8 + (u + 1))
                if u >= 2:
                    pe.wait_ge(S["o_evac"], j * 8 + (u - 1))
                for x in range(6):
                    v = vin[:, x if x < 4 else 4 * (x - 3) + r, HD * h2:HD * (h2 + 1)]
                    nx = nc.tensor.matmul(ps[:, 6 + o, 0:HD], pT[:, o, x * P:(x + 1) * P], v, start=x == 0,
                                          stop=x == 5)
                nx.then_inc(S["pv_done"], 1)
            pe.wait_ge(S["o_evac"], j * 8 + 8)
            for r in range(4):
                nx = nc.tensor.transpose(ps[:, 4, r * P:(r + 1) * P], oS[:, r, :], ident[:])
            nx.then_inc(S["ot_done"], 1)

        def transposes(b):
            pe.wait_ge(S["kc_in"], b * 112 + 112)
            for g in range(12):
                j, x = divmod(g, 3)
                bank = (3, 4, 5, 7)[g % 4]
                if g >= 4:
                    pe.wait_ge(S["ktd" if g % 2 == 0 else "kta"], b * 6 + (g // 2 - 1))
                cols = slice(j * P, (j + 1) * P)
                if x < 2:
                    for k in range(4):
                        nx = nc.tensor.transpose(ps[:, bank, k * P:(k + 1) * P], kc[:, 4 * x + k, cols], ident[:])
                else:
                    nc.tensor.transpose(ps[:, bank, 0:P], kc[:, 8, cols], ident[:])
                    nx = nc.tensor.transpose(ps[:, bank, P:P + 24], kn[:, cols], ident[0:24, 0:24])
                nx.then_inc(S["ktr"], 1)

        def sample_body(b, last):
            pe.wait_ge(S["q_ready"], b + 1)
            pe.wait_ge(S["ktd"], b * 6 + 6)
            pe.wait_ge(S["kta"], b * 6 + 6)
            for j in range(PAIRS):
                rows = slice(32 * j, 32 * j + 32)
                for bank, g, a, n in ((0, 1, C1, 512), (1, 2, C2, 512), (2, 0, C0, P)):
                    nx = nc.tensor.matmul(ps[rows, bank, 0:n], qs[:, 4 * g + j, :], kTs[:, j, a:a + n],
                                          start=True, stop=True, tile_position=(0, 32 * j))
                for g in range(3):
                    nx = nc.tensor.matmul(ps[rows, 2, P + g:P + 24:3], qs[:, 4 * g + j, :], kTs[:, j, CN + g:SC:3],
                                          start=True, stop=True, tile_position=(0, 32 * j))
            nx.then_inc(S["ss_mm"], 1)
            if not last:
                transposes(b + 1)
            pe.wait_ge(S["pn"], b + 1)
            if not last:
                pe.wait_ge(S["ktd"], b * 6 + 12)
                pe.wait_ge(S["kta"], b * 6 + 12)
            for k in range(10):
                n = P if k < 9 else 24
                nx = nc.tensor.transpose(ps[0:n, 3 + k // 4, k % 4 * P:(k % 4 + 1) * P], sS[:, k * P:k * P + n],
                                         ident[:])
                if k in (3, 7, 9):
                    nx.then_inc(S["ptr_mm"], 1)
            pe.wait_ge(S["vc_in"], b * 112 + 112)
            pe.wait_ge(S["ptr_a"], b * 2 + 2)
            pe.wait_ge(S["ptr_d"], b + 1)
            for j in range(PAIRS):
                cols = slice(j * P, (j + 1) * P)
                for k in range(10):
                    a = vc[:, k, cols] if k < 9 else vn[:, cols]
                    n = P if k < 9 else 24
                    nx = nc.tensor.matmul(ps[:, 6, 32 * j:32 * j + 32], a, ptS[0:n, k, 32 * j:32 * j + 32],
                                          start=k == 0, stop=k == 9)
            nx.then_inc(S["pv2"], 1)

        pe.wait_ge(S["ot_ready"], PAIRS)
        transposes(0)
        with pe.Fori(0, NB - 1) as b:
            sample_body(b, False)
        sample_body(NB - 1, True)

        for m in range(KD):
            s = m // 2
            pe.wait_ge(S["w_ready"], CB["wo"] + s + 1)
            if m >= 2:
                pe.wait_ge(S["x_ready"], KD * XV["ffn3_in"] + m - 1)
            for k in range(PAIRS):
                if m == 0:
                    pe.wait_ge(S["h_ready"], HB["wo"] + k + 1)
                cols = slice(k * 2 * P + m % 2 * P, k * 2 * P + m % 2 * P + P)
                nx = split_mm(halves(m % 2), wH[:, s % 2, cols], wL[:, s % 2, cols], oH[:, k], oL[:, k], k == 0,
                              k == PAIRS - 1)
            nx.then_inc(S["wo_even" if m % 2 == 0 else "pe_chunk"], 1)

        in_phase("ffn3_in")
        out_phase("ffn3_out", "ffn3_in")

        pe.wait_ge(S["sq_ready"], XV["final"] + 1)
        square_sum_tokens()
        pe.wait_ge(S["yg_ready"], KD)
        pe.wait_ge(S["x_ready"], KD * 7)
        ygf = yg[:].rearrange("p k a b -> p k (a b)")
        for t in range(TT):
            r = P if t < 4 else SMP
            if t >= 2:
                pe.wait_ge(S["y_ready"], t - 1)
            for k in range(KD):
                nx = nc.tensor.transpose(ps[0:r, 2 * (t % 2) + k // 4, k % 4 * P:(k % 4 + 1) * P],
                                         ygf[:, k, t * P:t * P + r], ident[:])
            nx.then_inc(S["yt"], 1)

    block_cm.__exit__(None, None, None)


_OUTS = (("y_prompt", (1, SEQ, D)), ("y_sample", (NB, NT, D)), ("conv_prompt", (1, 1, CW - 1, D)),
         ("conv_sample", (1, NB, CW - 1, D)), ("kv0_prompt", (1, 128, 2, HEADS, HD)),
         ("kv0_sample", (NB, 128, 2, HEADS, HD)), ("kv1_prompt", (1, SEQ, 2, HEADS, HD)),
         ("kv1_sample", (NB, 512, 2, HEADS, HD)), ("kv2_prompt", (1, SEQ, 2, HEADS, HD)),
         ("kv2_sample", (NB, PAST, 2, HEADS, HD)))


def kernel(**inputs):
    import concourse.bacc as bacc
    from concourse.bass_utils import run_bass_kernel_spmd

    nc = bacc.Bacc("TRN2", target_bir_lowering=False, num_devices=1)
    given = {name: np.ascontiguousarray(a) for name, a in inputs.items()}
    given.update(zip(("onehot", "onehot_sample", "unseen_sample", "unseen_rows"), bias_onehots()))
    ins = {n: nc.dram_tensor(f"in_{n}", a.shape, mybir.dt.from_np(a.dtype), kind="ExternalInput").ap()
           for n, a in given.items()}
    outs = {n: nc.dram_tensor(f"out_{n}", shape, f32, kind="ExternalOutput").ap() for n, shape in _OUTS}
    trunk_program(nc, ins, outs)
    r = run_bass_kernel_spmd(nc, [{f"in_{n}": a for n, a in given.items()}], core_ids=[0])
    return tuple(r.results[0][f"out_{n}"] for n, _ in _OUTS)
```

```python
import concourse.bass as bass
from concourse import mybir
import numpy as np

f32, f32r = mybir.dt.float32, mybir.dt.float32r
ALU, ACT, AX = mybir.AluOpType, mybir.ActivationFunctionType, mybir.AxisListType

P = 128
D, FF, SEQ, NB, NT = 1024, 2816, 512, 8, 8
SMP = NB * NT
TOK = SEQ + SMP
HALF = TOK // 2
KD, KF = D // P, FF // P
CW = 31
CD = 5
CP = KD - CD
HEADS, HD, AW = 8, 64, 512
PAIRS = HEADS * HD // P
WIN, DIL = (128, 512, 2048), (1, 4, 16)
CACHE = (128, 512, 1024)
EPS = 1e-6
NEG = -1e30
SLOT = KF // 2 * P
TT = 5

NORM, NORM_KV, NORM_F, B_PW1, B_DW, LN_G, LN_B, B_PW2, W_DW = 0, 6, 7, 8, 10, 11, 12, 13, 14
NPAR = W_DW + CW

R0_LEN = 4 * (P - 1) + SEQ + 3
R1_LEN = 2 * P - 1
R_LEN = R0_LEN + 2 * R1_LEN
T0W = SEQ + 3
C1, C2, C0, CN = 0, 512, 1024, 1152
SC = CN + 3 * NT

_W_PHASES = ("ffn0_in", "ffn0_out", "pw1", "pw2", "ffn1_in", "ffn1_out", "kv", "ffn2_in", "ffn2_out",
             "q", "wo", "ffn3_in", "ffn3_out")
CHUNKS = dict(pw1=16, pw2=8, kv=24, q=12, wo=4, **{f"ffn{n}_in": 2 * KF for n in range(4)},
              **{f"ffn{n}_out": 2 * KD for n in range(4)})
SIZE = dict(pw1=8 * P, pw2=8 * P, kv=8 * P, q=8 * P, wo=8 * P, **{f"ffn{n}_in": 8 * P for n in range(4)},
            **{f"ffn{n}_out": SLOT for n in range(4)})
MTILES = dict(pw1=16, pw2=0, kv=0, q=12, wo=0, **{f"ffn{n}_in": 2 * KF for n in range(4)},
              **{f"ffn{n}_out": 0 for n in range(4)})
CB = {ph: sum(CHUNKS[x] for x in _W_PHASES[:n]) for n, ph in enumerate(_W_PHASES)}
MB = {ph: sum(MTILES[x] for x in _W_PHASES[:n]) for n, ph in enumerate(_W_PHASES)}
NEXT_SIZE = {ph: SIZE[nx] for ph, nx in zip(_W_PHASES, _W_PHASES[1:])}
NEXT_SIZE[_W_PHASES[-1]] = None


def bucket(dist):
    d = np.maximum(dist, 1).astype(np.float32)
    large = 16 + (np.log(d / np.float32(16)) / np.float32(np.log(2048 / 16)) * 16).astype(np.int32)
    return np.where(dist < 16, dist, np.minimum(large, 31))


def bias_onehots():
    one = np.zeros((33, R_LEN), np.float32)

    def put(col, ok, dist):
        one[np.where(ok, bucket(np.where(ok, dist, 0)), 32), col] = 1.0

    y = np.arange(R0_LEN)
    n = SEQ - 1 - y
    put(y, (n >= 0) & (n <= WIN[0]), n)
    y = np.arange(R1_LEN)
    n = P - 1 - y
    put(R0_LEN + y, n >= 0, 4 * n)
    put(R0_LEN + R1_LEN + y, (n >= 0) & (n % 4 == 0), 4 * n)
    hot, bad = np.zeros((2, P, SC), np.float32), np.zeros((NT, SC), np.float32)
    for t in range(NT):
        dist = np.full(SC, -1)
        p = np.arange(CACHE[1])
        dist[C1:C2] = np.where((CACHE[1] + t - p) % DIL[1] == 0, CACHE[1] + t - p, -1)
        m, tt = np.arange(512) // 8, np.arange(512) % 8
        dist[C2:C0] = np.where(tt == t, PAST - 16 * m, -1)
        dist[C0:CN] = CACHE[0] + t - np.arange(P)
        for g in range(3):
            lag = t - np.arange(NT)
            dist[CN + g:SC:3] = np.where((lag >= 0) & (lag % DIL[g] == 0), lag, -1)
        top = np.full(SC, WIN[0])
        top[C1:C2], top[C2:C0] = WIN[1], WIN[2]
        ok = (dist >= 0) & (dist <= top)
        c = np.arange(SC)[ok]
        hot[t // 4, 32 * (t % 4) + bucket(dist[ok]), c] = 1.0
        bad[t, ~ok] = 1.0
    rows = np.zeros((NT, P), np.float32)
    for t in range(NT):
        for j in range(PAIRS):
            rows[t, [32 * j + t, 32 * j + NT + t]] = NEG
    return one, hot, bad, rows


PAST = 1024


class Steps:

    def __init__(self, engine, sem):
        self.engine, self.sem, self.n, self.i, self.per = engine, sem, 0, None, 0

    def mark(self, instruction):
        instruction.then_inc(self.sem, 1)
        self.n += 1

    def wait(self, back=0):
        at = self.n - back
        self.engine.wait_ge(self.sem, at if self.i is None else self.i * self.per + at)

    def loop(self, i, per):
        self.i, self.per, self.start = i, per, self.n

    def end(self, times):
        assert self.n - self.start == self.per, (self.n - self.start, self.per)
        self.n, self.i = self.start + self.per * times, None


def trunk_program(nc, I, O):
    sb0 = (nc.sbuf_usable_end - nc.sbuf_bytes_remaining + 63) // 64 * 64
    at = [sb0]

    def place(name, shape, dt=f32):
        t = nc.alloc_sbuf_tensor_at(name, shape, dt, offset=at[0])
        at[0] += (int(np.prod(shape[1:])) * 4 + 31) // 32 * 32
        return t

    xT = place("xT", [P, KD, 2, HALF])
    hH = place("hH", [P, KD, 2, HALF], f32r)
    hL = place("hL", [P, KD, 2, HALF], f32r)
    w_at = at[0]
    wst = place("wst", [P, 4, SLOT])
    wH = place("wH", [P, 2, SLOT], f32r)
    wL = place("wL", [P, 2, SLOT], f32r)
    rstd = place("rstd", [P, 2, HALF])
    par = place("par", [P, KD, NPAR])
    ident = place("ident", [P, P])
    ones = place("ones", [P, P])
    ta = place("ta", [P, 2, HALF])
    tb = place("tb", [P, 2, HALF])
    eps = place("eps", [P, 1])
    rstdT = place("rstdT", [P, 8])
    void = place("void", [P, 2])
    A0 = at[0]

    def region(*what):
        at[0] = A0
        got = [place(*w) for w in what]
        assert at[0] <= A_END, (what, at[0] - A0)
        return got

    A_END = nc.sbuf_usable_end
    actH, actL = region(("actH", [P, KF, 2, HALF], f32r), ("actL", [P, KF, 2, HALF], f32r))
    xr, parR = region(("xr", [P, TT, D]), ("parR", [NPAR, D]))
    UW = 30 + SEQ + NB * (30 + NT)
    wdH, wdL, stR, ucat, cT, cst, un, cH, cL = region(
        ("wdH", [P, CP, CW], f32r), ("wdL", [P, CP, CW]),
        ("stR", [120, 2, D]), ("ucat", [P, KD, UW]), ("cT", [P, KD, 2, HALF]), ("cst", [SMP, 2, D]),
        ("un", [P, KD, SMP]), ("cH", [P, KD, 2, HALF], f32r), ("cL", [P, KD, 2, HALF], f32r))
    c_end = at[0]
    at[0] = A0 + 2 * 384
    tS = place("tS", [P, 2, 4 * SMP])
    at[0] = A0 + 2 * 384 + 2 * D * 4
    Rsb, sbias0 = place("Rsb", [24, R_LEN]), place("sbias0", [P, SC])
    at[0] = sb0 + KD * TOK * 4
    relE, relq, E1, E2, Ebad, sel, selm = (
        place("relE", [33, 24]), place("relq", [P, 24]), place("E1", [33, R_LEN]), place("E2", [P, 2, SC]),
        place("Ebad", [NT, SC]), place("sel", [P, 2, 3, P]), place("selm", [NT, P]))
    assert at[0] <= sb0 + 3 * KD * TOK * 4
    diagH, diagL, uH, uL = [], [], [], []
    for slot, base in enumerate((c_end - 2 * KD * TOK * 4, sb0 + KD * TOK * 4)):
        at[0] = base
        diagH.append(place(f"diagH{slot}", [P, CW, P], f32r))
        diagL.append(place(f"diagL{slot}", [P, CW, P], f32r))
        uH.append(place(f"uH{slot}", [P, 30 + SEQ], f32r))
        uL.append(place(f"uL{slot}", [P, 30 + SEQ], f32r))
    kvst, = region(("kvst", [P, 2, TT, AW]))
    qT, oT, qc, vin, kin, bT, pT = region(
        ("qT", [P, 12, TOK]), ("oT", [P, PAIRS, 2, HALF]), ("qc", [P, 2, 3, 4, P]), ("vin", [P, 12, AW]),
        ("kin", [P, 12, P]), ("bT", [P, 2, T0W + 2 * P]), ("pT", [P, 2, 768]))
    at[0] = A0 + (12 * TOK + PAIRS * TOK) * 4
    kcB, vcB, kTs = place("kcB", [P, 9, AW]), place("vcB", [P, 9, AW]), place("kTs", [P, PAIRS, SC])
    qs, vnB, stS, oSs = place("qs", [P, 12, 32]), place("vnB", [24, AW]), place("stS", [P, 4]), place("oSs", [P, P])
    assert at[0] <= A_END
    at[0] = w_at
    vcA, vnA = place("vcA", [P, 9, AW]), place("vnA", [24, AW])
    assert at[0] <= w_at + 4 * SLOT * 4
    vc, vn = (vcA, vcB), (vnA, vnB)
    kn = [t[0:24].rearrange("p a b -> p (a b)")[:, 0:AW] for t in (ta, tb)]
    oH, oL = region(("oH", [P, PAIRS, 2, HALF], f32r), ("oL", [P, PAIRS, 2, HALF], f32r))
    H0 = sb0 + KD * TOK * 4
    at[0] = H0
    kT, sP, oS, stat = (place("kT", [P, 12, P]), place("sP", [P, 2, 768]), place("oS", [P, 4, P]),
                        place("stat", [P, 32]))
    prompt_end, at[0] = at[0], H0
    sS, ptS, sbias = place("sS", [P, SC]), place("ptS", [P, 10, P]), place("sbias", [P, SC])
    at[0] = max(at[0], prompt_end)
    kcA = place("kcA", [P, 9, AW])
    assert at[0] <= H0 + 2 * KD * TOK * 4
    kc = (kcA, kcB)
    at[0] = H0
    yg, yst = place("yg", [P, KD, 2, HALF]), place("yst", [P, 2, D])
    assert at[0] <= H0 + 2 * KD * TOK * 4

    ps = nc.alloc_psum_tensor("ps", [P, 8, 512], f32)

    def pair(p):
        return ps[:, 2 * p:2 * p + 2, 0:HALF]

    def tile(t, k):
        return t[:, k] if isinstance(k, int) else t[:, bass.ds(k, 1)].rearrange("p o a b -> p (o a) b")

    def tokens(t, k=None):
        return (t[:] if k is None else tile(t, k)).rearrange("p a b -> p (a b)")

    def column(k, row):
        return par[:, k:k + 1, row] if isinstance(k, int) else par[:, bass.ds(k, 1), row]

    def pair_queries(copy, j, h2):
        q = slice(HD * h2, HD * (h2 + 1))
        src = qT[q, :, 0:SEQ].rearrange("p (g j) (a r) -> p g j r a", g=3, r=4)
        src = src[:, :, j] if isinstance(j, int) else src[:, :, bass.ds(j, 1)].rearrange("p g o r a -> p g (o r) a")
        for g in range(3):
            nx = copy(qc[q, h2, g, :, ::-1], src[:, g])
        return nx

    rvec = nc.dram_tensor("rvec", (24, R_LEN), f32, kind="Internal").ap()
    sbd = nc.dram_tensor("sbd", (P, SC), f32, kind="Internal").ap()
    kvs = nc.dram_tensor("kvs", (TOK, 6 * AW), f32, kind="Internal").ap()
    kvs3 = kvs.rearrange("t (g x) -> (t g) x", g=3)

    names = """par_in x_in0 x_in1 bias_in st_in rvec_out sbd_out sbias_in kv_out0 kv_out1 kv_copy cache_copy
        state_copy conv_out y_out0 y_out1 w_h w_ready pe_chunk wo_even evac x_ready h_h h_ready
        sq_ready ss_done std_ready ssT_done stdT_ready silu_done act_in act_h act_ready ident_ready
        consts_ready par_t par_ready x_t b_mm b_ev sel_ready glu_done st_t st_ready u_ready u_t u_ev
        c_ready mu_mm cc_ready csq_ready var_mm lnstd_ready ln_in kv_evac wd_h wd_ready diag_h
        diag_l uh_ready ul_ready ul7_ready conv_mm cp_ready cs_ready un_ready q_ready k_in v_in
        b_in0 b_in1 kt_tr kt_d kt_a qc_zero qc_a qc_d s_done s_evac sm_ready p_ready pt_done
        pt_ready pv_done o_evac ot_done ot_ready kc_in0 kc_in1 vc_in0 vc_in1 ktr ktd kta ss_mm sm2
        p2 os_ready ot2 ptr_d ptr_a ptr_mm pv2 o2 yg_ready yt y_ready dve_self act_self pool_self""".split()
    S = {n: nc.alloc_semaphore(n) for n in names}
    w_in = [nc.alloc_semaphore(f"w_in{s}") for s in range(4)]

    FB = {f"ffn{n}_in": KF * n for n in range(4)}
    HB, hn = {}, 0
    for name, k in (("ffn0_in", 8), ("pw1", 8), ("pw2", 8), ("ffn1_in", 8), ("kv", 8), ("ffn2_in", 8), ("q", 8),
                    ("wo", 4), ("ffn3_in", 8)):
        HB[name] = hn
        hn += k
    XV = dict(ffn0_in=0, pw1=1, ffn1_in=2, kv=3, ffn2_in=3, q=4, ffn3_in=5, final=6)
    GAIN = dict(ffn0_in=NORM, pw1=NORM + 1, ffn1_in=NORM + 2, kv=NORM_KV, ffn2_in=NORM + 3, q=NORM + 4,
                ffn3_in=NORM + 5, final=NORM_F)
    AFTER = dict(ffn0_out="pw1", pw2="ffn1_in", ffn1_out="kv", ffn2_out="q", wo="ffn3_in", ffn3_out="final")
    ROUND = dict(ffn0_in=1, pw1=2, ffn1_in=3, ffn2_in=4, q=5, ffn3_in=6)
    ROUNDT = dict(kv=1, final=2)

    block_cm = nc.Block()
    block = block_cm.__enter__()

    w_view = {}
    for n in range(4):
        w_view[f"ffn{n}_in"] = I["ffn_w_in"][n // 2, n % 2].rearrange("(k p) n -> p k n", p=P)
        w_view[f"ffn{n}_out"] = I["ffn_w_out"][n // 2, n % 2].rearrange("(k p) n -> p k n", p=P)
    w_view["pw1"] = I["conv_w_pw1"][0].rearrange("(k p) n -> p k n", p=P)
    w_view["pw2"] = I["conv_w_pw2"][0].rearrange("(k p) n -> p k n", p=P)
    w_view["kv"] = I["w_kv"].rearrange("(k p) n -> p k n", p=P)
    w_view["q"] = I["attn_w_q"][0].rearrange("(k p) n -> p k n", p=P)
    w_view["wo"] = I["attn_w_o"][0].rearrange("(k p) n -> p k n", p=P)

    def chunk_source(sp, ph, i, s):
        w = w_view[ph]

        def at_col(x):
            return x if isinstance(x, int) else sp.snap(x)

        if ph.endswith("_in") or ph == "pw1":
            half = FF if ph != "pw1" else D
            return w[:, :, bass.ds(at_col(i * 2 * P + s // 2 * P + s % 2 * half), P)]
        if ph.endswith("_out"):
            return w[:, s % 2 * (KF // 2):(s % 2 + 1) * (KF // 2), bass.ds(at_col(i * 2 * P + s // 2 * P), P)]
        if ph in ("pw2", "q"):
            return w[:, :, bass.ds(at_col(i * 4 * P + s * P), P)]
        if ph == "kv":
            return w[:, 2 * s:2 * s + 2, bass.ds(at_col(i * AW), AW)]
        return w[:, :, bass.ds(at_col(i * 8 * P + s * 2 * P), 2 * P)]

    @block.sync
    def _(sp):
        xp = I["x_prompt"][0].rearrange("(k p) n -> p k n", p=P)
        xs = I["x_sample"].rearrange("b t n -> (b t) n")

        def x_half(h):
            cols = slice(h * (D // 2), (h + 1) * (D // 2))
            sp.dma_start(xr[:, 0:4, cols], xp[:, :, cols]).then_inc(S[f"x_in{h}"], 16)
            sp.dma_start(xr[0:SMP, 4, cols], xs[:, cols]).then_inc(S[f"x_in{h}"], 16)

        x_half(0)
        sp.dma_start(parR[NORM:NORM + 6, :], I["norms"].rearrange("a b n -> (a b) n")).then_inc(S["par_in"], 16)
        sp.dma_start(parR[NORM_KV:NORM_KV + 1, :], I["norm_kv"][None, :]).then_inc(S["par_in"], 16)
        sp.dma_start(parR[NORM_F:NORM_F + 1, :], I["norm_final"][None, :]).then_inc(S["par_in"], 16)
        sp.dma_start(parR[B_PW1:B_PW1 + 2, :], I["conv_b_pw1"].rearrange("a (b n) -> (a b) n", b=2)
                     ).then_inc(S["par_in"], 16)
        for row, name in ((B_DW, "conv_b_dw"), (LN_G, "conv_ln_g"), (LN_B, "conv_ln_b"), (B_PW2, "conv_b_pw2")):
            sp.dma_start(parR[row:row + 1, :], I[name]).then_inc(S["par_in"], 16)
        sp.dma_start(parR[W_DW:NPAR, :], I["conv_w_dw"][0]).then_inc(S["par_in"], 16)
        x_half(1)

        def chunk(ph, i, s, first=False):
            src = chunk_source(sp, ph, i, s)
            if not first:
                sp.wait_ge(S["w_ready"], i * 4 + (CB[ph] + s - 3))
            k, n = src.shape[1], src.shape[2]
            sp.dma_start(wst[:, s, 0:k * n].rearrange("p (k n) -> p k n", n=n), src).then_inc(w_in[s], 16)

        for s in range(4):
            chunk("ffn0_in", 0, s, first=True)

        def stream(ph, start=0):
            n = CHUNKS[ph] // 4
            if n - start == 1:
                for s in range(4):
                    chunk(ph, start, s)
            else:
                with sp.Fori(start, n) as i:
                    for s in range(4):
                        chunk(ph, i, s)

        stream("ffn0_in", 1)
        stream("ffn0_out")
        for s in range(4):
            chunk("pw1", 0, s)
        sp.wait_ge(S["pe_chunk"], CB["pw1"])
        sp.dma_start(stR[:], I["state_conv"][0].rearrange("(h b) t n -> (b t) h n", h=2)).then_inc(S["st_in"], 16)
        stream("pw1", 1)
        for s in range(4):
            chunk("pw2", 0, s)
        sp.wait_ge(S["conv_mm"], 2)
        sp.dma_start(relE[0:32, :], I["rel_bias"]).then_inc(S["bias_in"], 16)
        for q in range(4):
            sp.dma_start(relq[32 * q:32 * q + 32, :], I["rel_bias"]).then_inc(S["bias_in"], 16)
        sp.dma_start(E1[:], I["onehot"]).then_inc(S["bias_in"], 16)
        sp.dma_start(E2[:], I["onehot_sample"].rearrange("h p c -> p h c")).then_inc(S["bias_in"], 16)
        sp.dma_start(Ebad[:], I["unseen_sample"]).then_inc(S["bias_in"], 16)
        sp.dma_start(selm[:], I["unseen_rows"]).then_inc(S["bias_in"], 16)
        stream("pw2", 1)
        sp.wait_ge(S["b_ev"], 6)
        sp.dma_start(rvec, Rsb[:]).then_inc(S["rvec_out"], 16)
        sp.dma_start(sbd, sbias0[:]).then_inc(S["sbd_out"], 16)

        for ph in ("ffn1_in", "ffn1_out", "kv", "ffn2_in", "ffn2_out"):
            stream(ph)
        for s in range(4):
            chunk("q", 0, s)
        sp.wait_ge(S["rvec_out"], 16)
        sp.wait_ge(S["sbd_out"], 16)
        sp.wait_ge(S["kv_out0"], 16 * 6)
        sp.wait_ge(S["kv_out1"], 16 * 6)
        sp.wait_ge(S["pe_chunk"], CB["q"])
        rt = rvec.tensor
        def pair_keys(j):
            for g in range(3):
                src = kvs[0:SEQ, 2 * g * AW + j * P:2 * g * AW + (j + 1) * P]
                src = src.rearrange("(k p) n -> p k n", p=P) if g == 0 else src.rearrange("(a r) n -> a r n", r=4)
                sp.dma_start(kin[:, 4 * g:4 * g + 4, :], src).then_inc(S["k_in"], 16)

        def head_bias(j, h2):
            for g, (off, step, col, n) in enumerate(((0, 4, 0, T0W), (R0_LEN, 1, T0W, P),
                                                     (R0_LEN + R1_LEN, 1, T0W + P, P))):
                src = bass.AP(rt, (8 * g + 2 * j + h2) * R_LEN + off, [[step, P], [1, n]])
                sp.dma_start(bT[:, h2, col:col + n], src).then_inc(S[f"b_in{h2}"], 16)

        pair_keys(0)
        head_bias(0, 0)
        head_bias(0, 1)
        for g in range(3):
            src = kvs[0:SEQ, (2 * g + 1) * AW:(2 * g + 2) * AW]
            src = src.rearrange("(k p) n -> p k n", p=P) if g == 0 else src.rearrange("(a r) n -> a r n", r=4)
            sp.dma_start(vin[:, 4 * g:4 * g + 4, :], src).then_inc(S["v_in"], 16)
        stream("q", 1)

        c512 = I["cache_kv_w512"].rearrange("b (k p) v h d -> b p k v (h d)", p=P)
        c128 = I["cache_kv_w128"].rearrange("b p v h d -> b p v (h d)")
        c2048 = I["cache_kv_w2048"].rearrange("b (k m t) v h d -> b k m t v (h d)", k=4, t=16)

        def cache_rows(b, kv):
            dst, new, sem = ((kc[b % 2], kn[b % 2], f"kc_in{b % 2}"), (vc[b % 2], vn[b % 2][:], f"vc_in{b % 2}"))[kv]
            sp.dma_start(dst[:, 0:4, :], c512[b, :, :, kv, :]).then_inc(S[sem], 16)
            for k in range(4):
                sp.dma_start(dst[:, 4 + k, :], c2048[b, k, :, 0:NT, kv, :]).then_inc(S[sem], 16)
            sp.dma_start(dst[:, 8, :], c128[b, :, kv, :]).then_inc(S[sem], 16)
            r0 = (SEQ + NT * b) * 3
            sp.dma_start(new, kvs3[r0:r0 + 24, kv * AW:(kv + 1) * AW]).then_inc(S[sem], 16)

        for j in range(1, PAIRS):
            sp.wait_ge(S["kt_tr"], 3 * j)
            pair_keys(j)
            if j == 1:
                sp.wait_ge(S["pe_chunk"], CB["wo"])
                sp.wait_ge(S["sq_ready"], 5)
                cache_rows(0, 0)
                sp.wait_ge(S["w_ready"], CB["wo"])
                cache_rows(0, 1)
            for h2 in range(2):
                sp.wait_ge(S["s_evac"], 8 * j + h2)
                head_bias(j, h2)
        sp.wait_ge(S["ot_ready"], PAIRS)
        sp.dma_start(sbias[:], sbd).then_inc(S["sbias_in"], 16)
        cache_rows(1, 0)
        cache_rows(1, 1)
        for b in range(2, NB):
            sp.wait_ge(S["ktr"], 12 * (b - 1))
            cache_rows(b, 0)
            sp.wait_ge(S["pv2"], b - 1)
            cache_rows(b, 1)
        sp.wait_ge(S["pv2"], NB - 1)
        stream("wo")
        stream("ffn3_in")
        stream("ffn3_out")
        sp.wait_ge(S["kv_copy"], 16 * 6)
        sp.wait_ge(S["cache_copy"], 16 * 24)
        sp.wait_ge(S["state_copy"], 16)
        sp.wait_ge(S["conv_out"], 16 * 9)
        for t in range(TT):
            sp.wait_ge(S["y_ready"], t + 1)
            out = S[f"y_out{t % 2}"]
            if t < 4:
                sp.dma_start(O["y_prompt"][0, t * P:(t + 1) * P, :], yst[:, t % 2, :]).then_inc(out, 16)
            else:
                sp.dma_start(O["y_sample"].rearrange("b t n -> (b t) n"), yst[0:SMP, t % 2, :]
                             ).then_inc(out, 16)
        sp.wait_ge(S["y_out0"], 16 * 3)
        sp.wait_ge(S["y_out1"], 16 * 2)

    @block.gpsimd
    def _(pool):
        me = Steps(pool, S["pool_self"])
        me.mark(nc.gpsimd.memset(ident[:], 0.0))
        me.wait()
        nc.gpsimd.affine_select(out=ident[:], in_=ident[:], compare_op=ALU.not_equal, fill=1.0, base=0,
                                pattern=[[-1, P]], channel_multiplier=1).then_inc(S["ident_ready"], 1)

        def squares(version):
            for k in range(KD):
                pool.wait_ge(S["x_ready"], KD * version + k + 1)
                if k == 0:
                    me.mark(nc.gpsimd.tensor_tensor(tokens(tb), tokens(xT, k), tokens(xT, k), ALU.mult))
                    continue
                me.mark(nc.gpsimd.tensor_tensor(tokens(ta), tokens(xT, k), tokens(xT, k), ALU.mult))
                me.wait()
                add = nc.gpsimd.tensor_tensor(tokens(tb), tokens(tb), tokens(ta), ALU.add)
                if k < KD - 1:
                    me.mark(add)
                    me.wait()
                else:
                    add.then_inc(S["sq_ready"], 1)

        def shift_cache(g, entries=range(NB), ph=None, start=0, every=0):
            for at_, b in enumerate(entries):
                if ph:
                    pool.wait_ge(S["pe_chunk"], CB[ph] + start + at_ * every)
                n = CACHE[g] - NT
                src = I[f"cache_kv_w{WIN[g]}"][b, NT:CACHE[g]].rearrange("t v h d -> t (v h d)")
                dst = O[f"kv{g}_sample"][b, 0:n].rearrange("t v h d -> t (v h d)")
                pool.dma_start(dst, src).then_inc(S["cache_copy"], 16)

        pool.wait_ge(S["consts_ready"], 1)
        squares(0)
        shift_cache(2, range(0, 4), "ffn0_in", 8, 10)
        squares(1)
        shift_cache(0, ph="pw1", start=1)
        pool.dma_start(O["conv_sample"][0, :, 0:CW - 1 - NT], I["state_conv"][0, :, NT:]).then_inc(S["state_copy"], 16)

        def diag_low(n):
            nc.gpsimd.tensor_tensor(diagL[n % 2][:], ident[:].rearrange("p (o c) -> p o c", o=1).broadcast_to([P, CW, P]),
                                    wdL[:, n, :].rearrange("p (k o) -> p k o", o=1).broadcast_to([P, CW, P]),
                                    ALU.mult).then_inc(S["diag_l"], 1)

        def u_low(n):
            pool.wait_ge(S["uh_ready"], n + 1)
            nc.gpsimd.tensor_tensor(uL[n % 2][:], ucat[:, CD + n, 0:30 + SEQ], uH[n % 2][:].bitcast(f32),
                                    ALU.subtract).then_inc(S["ul_ready"], 1)

        def sample_taps(q):
            tiles = slice(4 * q, 4 * q + 4)
            u4 = ucat[:, tiles, 30 + SEQ:UW].rearrange("p k (b t) -> p k b t", b=NB)
            c = cT[:, tiles].rearrange("p k a b -> p k (a b)")[:, :, SEQ:TOK]

            def row(r):
                return par[:, tiles, r:r + 1].rearrange("p k (x y) -> p k x y", y=1).broadcast_to([P, 4, NB, NT])

            def product(k):
                me.mark(nc.gpsimd.tensor_tensor(tS[:, k % 2, :].rearrange("p (k b t) -> p k b t", k=4, b=NB),
                                                u4[:, :, :, k:k + NT], row(W_DW + k), ALU.mult))

            def term(k):
                return tS[:, k % 2, :].rearrange("p (k x) -> p k x", k=4)

            pool.wait_ge(S["u_ready"], 4 * q + 4)
            if q:
                pool.wait_ge(S["cs_ready"], q)
            product(0)
            for k in range(CW):
                if k < CW - 1:
                    if k:
                        me.wait()
                    product(k + 1)
                if k == 0:
                    me.wait(1)
                    nx = nc.gpsimd.tensor_tensor(
                        c, term(0), par[:, tiles, B_DW:B_DW + 1].broadcast_to([P, 4, SMP]), ALU.add)
                else:
                    me.wait(1 if k < CW - 1 else 0)
                    nx = nc.gpsimd.tensor_tensor(c, c, term(k), ALU.add)
                if k < CW - 1:
                    me.mark(nx)
                else:
                    nx.then_inc(S["cs_ready"], 1)

        pool.wait_ge(S["pe_chunk"], CB["pw1"])
        pool.wait_ge(S["wd_ready"], 1)
        diag_low(0)
        pool.wait_ge(S["st_ready"], KD)
        sample_taps(0)
        u_low(0)
        pool.wait_ge(S["pe_chunk"], CB["pw2"])
        diag_low(1)
        u_low(1)
        sample_taps(1)
        pool.wait_ge(S["conv_mm"], 2)
        pool.wait_ge(S["cs_ready"], 2)
        me.mark(nc.gpsimd.memset(relE[32:33, :], NEG))
        me.wait()
        me.mark(nc.gpsimd.memset(sel[:], 0.0))
        me.wait()
        pool.wait_ge(S["bias_in"], 16 * 9)
        for tg in range(2):
            for t4 in range(4):
                t = 4 * tg + t4
                q = slice(32 * t4, 32 * t4 + 32)
                dst = sel[q, tg, :, :].rearrange("p g (j x) -> p g j x", j=PAIRS)[:, :, :, t:t + NT + 1:NT]
                src = relq[q, :].rearrange("p (g j x) -> p g j x", g=3, j=PAIRS)
                nx = nc.gpsimd.tensor_copy(dst.rearrange("p g j x -> p (g j) x"), src.rearrange("p g j x -> p (g j) x"))
        nx.then_inc(S["sel_ready"], 1)
        for b in range(NB):
            if b == 0:
                pool.wait_ge(S["u_ev"], 4)
                pool.dma_start(O["conv_prompt"][0, 0], cst[0:30, 0, :]).then_inc(S["conv_out"], 16)
            pool.dma_start(O["conv_sample"][0, b, CW - 1 - NT:], cst[b * NT:(b + 1) * NT, 1, :]
                           ).then_inc(S["conv_out"], 16)
        squares(2)
        shift_cache(2, range(4, 8), "ffn1_in", 4, 10)
        squares(3)
        for n in range(6):
            pool.wait_ge(S["kv_evac"], 5 * n + 10)
            cols = slice(n * AW, (n + 1) * AW)
            out = S[f"kv_out{n % 2}"]
            pool.dma_start(kvs[0:SEQ, cols].rearrange("(k p) n -> p k n", p=P), kvst[:, n % 2, 0:4, :]).then_inc(out, 16)
            pool.dma_start(kvs[SEQ:TOK, cols], kvst[0:SMP, n % 2, 4, :]).then_inc(out, 16)
        pool.wait_ge(S["kv_out0"], 16 * 6)
        pool.wait_ge(S["kv_out1"], 16 * 6)
        for g in range(3):
            keep = min(WIN[g], SEQ)
            cols = slice(2 * g * AW, 2 * (g + 1) * AW)
            pool.dma_start(O[f"kv{g}_prompt"][0].rearrange("t v h d -> t (v h d)"), kvs[SEQ - keep:SEQ, cols]
                           ).then_inc(S["kv_copy"], 16)
            pool.dma_start(O[f"kv{g}_sample"][:, CACHE[g] - NT:].rearrange("b t v h d -> b t (v h d)"),
                           kvs[SEQ:TOK, cols].rearrange("(b t) n -> b t n", t=NT)).then_inc(S["kv_copy"], 16)
        shift_cache(1, ph="ffn2_in", start=2, every=5)
        squares(4)
        pool.wait_ge(S["pe_chunk"], CB["q"])
        nc.gpsimd.memset(qc[:], 0.0).then_inc(S["qc_zero"], 1)
        squares(5)
        squares(6)

    @block.scalar
    def _(act):
        me = Steps(act, S["act_self"])

        def split_high(c, s, size):
            if size is None:
                return
            if isinstance(c, int) and c < 2:
                pass
            else:
                act.wait_ge(S["pe_chunk"], c - 1)
            act.wait_ge(w_in[s], (c - s) * 4 + 16)
            nc.scalar.copy(wH[:, s % 2, 0:size], wst[:, s, 0:size]).then_inc(S["w_h"], 1)

        def gain_high(ph, k):
            act.wait_ge(S["x_ready"], KD * XV[ph] + k + 1)
            g = column(k, GAIN[ph])
            if ph == "final":
                nc.scalar.mul(tokens(yg, k), tokens(xT, k), g).then_inc(S["yg_ready"], 1)
            else:
                nc.scalar.mul(tokens(hH, k), tokens(xT, k), g).then_inc(S["h_h"], 1)

        def std(ph):
            act.wait_ge(S["ss_done"], ROUND[ph])
            nc.scalar.activation(rstd[:], pair(1), ACT.Sqrt, scale=1.0 / D, bias=eps[:, 0:1]
                                 ).then_inc(S["std_ready"], 1)

        def std_tokens(ph):
            act.wait_ge(S["ssT_done"], ROUNDT[ph])
            nc.scalar.activation(rstdT[:, 0:4], ps[:, 6, 0:4], ACT.Sqrt, scale=1.0 / D, bias=eps[:, 0:1])
            nc.scalar.activation(rstdT[0:SMP, 4:5], ps[0:SMP, 6, 4:5], ACT.Sqrt, scale=1.0 / D,
                                 bias=eps[0:SMP, 0:1]).then_inc(S["stdT_ready"], 1)

        def ffn_in(ph):
            std(ph)
            n = CHUNKS[ph] // 4

            def body(i, last):
                for u in range(2):
                    f = i * 2 + u
                    size = NEXT_SIZE[ph] if last and u else SIZE[ph]
                    split_high(i * 4 + (CB[ph] + 2 * u + 2), (2 * u + 2) % 4, size)
                    act.wait_ge(S["evac"], i * 4 + (MB[ph] + 2 * u + 5))
                    nc.scalar.activation(ta[:], ta[:], ACT.Silu).then_inc(S["silu_done"], 1)
                    split_high(i * 4 + (CB[ph] + 2 * u + 3), (2 * u + 3) % 4, size)
                    act.wait_ge(S["act_in"], f + (FB[ph] + 1))
                    nc.scalar.copy(tile(actH, f), tb[:]).then_inc(S["act_h"], 1)

            with act.Fori(0, n - 1) as i:
                body(i, False)
            body(n - 1, True)

        def ffn_out(ph):
            def body(i, last):
                c, size = i * 4 + CB[ph], NEXT_SIZE[ph] if last else SIZE[ph]
                split_high(c + 2, 2, SIZE[ph])
                split_high(c + 3, 3, SIZE[ph])
                gain_high(AFTER[ph], i * 2)
                split_high(c + 4, 0, size)
                split_high(c + 5, 1, size)
                gain_high(AFTER[ph], i * 2 + 1)

            with act.Fori(0, 3) as i:
                body(i, False)
            body(3, True)

        split_high(0, 0, SIZE["ffn0_in"])
        split_high(1, 1, SIZE["ffn0_in"])
        act.wait_ge(S["par_ready"], 1)
        for k in range(KD):
            gain_high("ffn0_in", k)
        ffn_in("ffn0_in")
        ffn_out("ffn0_out")
        std("pw1")
        nc.scalar.copy(wdH[:], par[:, CD:KD, W_DW:NPAR]).then_inc(S["wd_h"], 1)

        def diagonals(out, w, n, a, b):
            for k in range(a, b):
                nx = nc.scalar.mul(out[n % 2][:, k, :], ident[:], w[:, n, k:k + 1])
            return nx

        def u_high(n):
            act.wait_ge(S["u_ready"], CD + n + 1)
            nc.scalar.copy(uH[n % 2][:], ucat[:, CD + n, 0:30 + SEQ]).then_inc(S["uh_ready"], 1)

        def conv_out(n):
            act.wait_ge(S["conv_mm"], n + 1)
            nc.scalar.activation(tokens(cT, CD + n)[:, 0:SEQ], ps[:, 2 + n, :], ACT.Identity,
                                 bias=par[:, CD + n:CD + n + 1, B_DW]).then_inc(S["cp_ready"], 1)

        high = wdH[:].bitcast(f32)
        for ct in range(KD):
            for v in range(2):
                c = CB["pw1"] + 2 * ct + v + 2
                split_high(c, c % 4, NEXT_SIZE["pw1"] if ct == KD - 1 else SIZE["pw1"])
                if v == 0 and ct < 4:
                    act.wait_ge(S["wd_h"], 1)
                    nx = diagonals(diagH, high, 0, 8 * ct, min(CW, 8 * ct + 8))
                    if ct == 3:
                        nx.then_inc(S["diag_h"], 1)
            act.wait_ge(S["evac"], MB["pw1"] + 2 * ct + 6)
            nc.scalar.activation(tb[:], tb[:], ACT.Sigmoid, bias=column(ct, B_PW1 + 1)).then_inc(S["glu_done"], 1)
            if ct == CD + 1:
                u_high(0)
        act.wait_ge(S["pe_chunk"], CB["pw2"])
        u_high(1)
        diagonals(diagH, high, 1, 0, CW).then_inc(S["diag_h"], 1)
        conv_out(0)
        u_high(2)
        diagonals(diagH, high, 2, 0, CW)
        act.wait_ge(S["wd_ready"], 1)
        diagonals(diagL, wdL, 2, 0, CW).then_inc(S["diag_h"], 1)
        conv_out(1)
        conv_out(2)
        for n in range(4):
            rows = 30 if n < 2 else SMP
            act.wait_ge(S["u_t"], n + 1)
            nc.scalar.copy(cst[0:rows, n // 2, n % 2 * 512:(n % 2 + 1) * 512], ps[0:rows, 4 + n, :]
                           ).then_inc(S["u_ev"], 1)
        act.wait_ge(S["b_mm"], 1)
        act.wait_ge(S["c_ready"], CD)
        act.wait_ge(S["cs_ready"], 2)
        for n in range(3):
            a, b = n * 512, min(R_LEN, (n + 1) * 512)
            nc.scalar.copy(Rsb[:, a:b], ps[0:24, 4 + n, 0:b - a]).then_inc(S["b_ev"], 1)
        for k in range(KD):
            act.wait_ge(S["cc_ready"], k + 1)
            if k >= 2:
                act.wait_ge(S["var_mm"], k - 1)
            nc.scalar.activation((ta, tb)[k % 2][:], cT[:, k], ACT.Square).then_inc(S["csq_ready"], 1)
        act.wait_ge(S["var_mm"], KD)
        nc.scalar.activation(rstd[:], pair(1), ACT.Sqrt, scale=1.0 / D, bias=eps[:, 0:1]
                             ).then_inc(S["lnstd_ready"], 1)
        for k in range(KD):
            act.wait_ge(S["ln_in"], k + 1)
            me.mark(nc.scalar.activation(cT[:, k], cT[:, k], ACT.Silu, scale=par[:, k:k + 1, LN_G],
                                         bias=par[:, k:k + 1, LN_B]))
            me.wait()
            nc.scalar.copy(cH[:, k], cT[:, k]).then_inc(S["h_h"], 1)
        for m in range(KD):
            c = CB["pw2"] + m + 2
            split_high(c, c % 4, SIZE["pw2"] if m < KD - 2 else NEXT_SIZE["pw2"])
            gain_high("ffn1_in", m)
            if m == 2:
                act.wait_ge(S["b_mm"], 2)
                for n, (a, b) in enumerate(((C1, C2), (C2, C0), (C0, SC))):
                    nc.scalar.copy(sbias0[:, a:b], ps[:, (7, 4, 5)[n], 0:b - a]).then_inc(S["b_ev"], 1)
        act.wait_ge(S["conv_out"], 16 * 9)
        act.wait_ge(S["rvec_out"], 16)
        act.wait_ge(S["sbd_out"], 16)
        ffn_in("ffn1_in")
        ffn_out("ffn1_out")
        std_tokens("kv")
        with act.Fori(0, 5) as i:
            for s in range(4):
                split_high(i * 4 + (CB["kv"] + 2 + s), (s + 2) % 4, SIZE["kv"])
        for s in range(4):
            split_high(CB["kv"] + 20 + 2 + s, (s + 2) % 4, SIZE["kv"] if s < 2 else NEXT_SIZE["kv"])
        act.wait_ge(S["pe_chunk"], CB["ffn2_in"])
        for k in range(KD):
            gain_high("ffn2_in", k)
        act.wait_ge(S["kv_out0"], 16 * 6)
        act.wait_ge(S["kv_out1"], 16 * 6)
        ffn_in("ffn2_in")
        ffn_out("ffn2_out")
        std("q")
        for c in range(12):
            split_high(CB["q"] + c + 2, (c + 2) % 4, SIZE["q"] if c < 10 else None)
        def keys(j, g):
            act.wait_ge(S["kt_tr"], j * 3 + (g + 1))
            nc.scalar.copy(kT[:, 4 * g:4 * g + 4, :].rearrange("p x n -> p (x n)"), ps[:, 7, :]
                           ).then_inc(S["kt_a"], 1)

        def exp(j, u):
            act.wait_ge(S["sm_ready"], j * 8 + (u + 1))
            o, c = u % 2, u % 8
            nc.scalar.activation(sP[:, o, :], sP[:, o, :], ACT.Exp, bias=stat[:, c:c + 1],
                                 accum_out=stat[:, 8 + c:9 + c]).then_inc(S["p_ready"], 1)

        def prompt_pair(j, last):
            for u in range(8):
                act.wait_ge(S["pt_done"], j * 8 + (u + 1))
                act.wait_ge(S["pv_done"], j * 8 + (u + 1))
                nc.scalar.copy(pT[:, u % 2, :], ps[:, 4:6, :].rearrange("p a b -> p (a b)")[:, 0:768]
                               ).then_inc(S["pt_ready"], 1)
                if u in (5, 6) and not last:
                    keys(j + 1, 2 * (u - 5))
                if u < 7 or not last:
                    exp(j, u + 1)
                if u == 5 and not last:
                    act.wait_ge(S["s_done"], j * 8 + 8)
                    pair_queries(nc.scalar.copy, j + 1, 0).then_inc(S["qc_a"], 1)

        act.wait_ge(S["qc_zero"], 1)
        act.wait_ge(S["evac"], MB["q"] + 12 + 4)
        pair_queries(nc.scalar.copy, 0, 0).then_inc(S["qc_a"], 1)
        keys(0, 0)
        keys(0, 2)
        exp(0, 0)
        with act.Fori(0, PAIRS - 1) as j:
            prompt_pair(j, False)
        prompt_pair(PAIRS - 1, True)
        def kt_copies(i, u, groups):
            for g in groups:
                act.wait_ge(S["ktr"], i * 24 + (12 * u + g + 1))
                jj, x = divmod(g, 3)
                a, n = ((C1, 512), (C2, 512), (C0, SC - C0))[x]
                nc.scalar.copy(kTs[:, jj, a:a + n], ps[:, (3, 4, 5, 7)[g % 4], 0:n]).then_inc(S["kta"], 1)

        early, late = (0, 1, 2, 3), (8, 9)

        def sample_body(i, last):
            for u in range(2):
                if not (last and u):
                    kt_copies(i, u + 1, early)
                act.wait_ge(S["sm2"], i * 2 + (u + 1))
                nc.scalar.activation(sS[:], sS[:], ACT.Exp, bias=stS[:, 0:1], accum_out=stS[:, 1:2]
                                     ).then_inc(S["p2"], 1)
                if not (last and u):
                    kt_copies(i, u + 1, late)
                for x in range(2):
                    act.wait_ge(S["ptr_mm"], i * 6 + (3 * u + x + 1))
                    nc.scalar.copy(ptS[:, 4 * x:4 * x + 4, :].rearrange("p a b -> p (a b)"), ps[:, 3 + x, :]
                                   ).then_inc(S["ptr_a"], 1)

        kt_copies(0, 0, early + late)
        with act.Fori(0, NB // 2 - 1) as i:
            sample_body(i, False)
        sample_body(NB // 2 - 1, True)
        for c in range(2):
            split_high(CB["wo"] + c, c, SIZE["wo"])
        act.wait_ge(S["o2"], NB)
        for k in range(PAIRS):
            nc.scalar.copy(oH[:, k], oT[:, k]).then_inc(S["h_h"], 1)
        for m in range(KD):
            if m % 2 == 0:
                c = m // 2 + 2
                split_high(CB["wo"] + c, c % 4, SIZE["wo"] if c < 4 else NEXT_SIZE["wo"])
            gain_high("ffn3_in", m)
        ffn_in("ffn3_in")
        ffn_out("ffn3_out")
        std_tokens("final")

    @block.vector
    def _(dve):
        me = Steps(dve, S["dve_self"])

        def split_low(c, s, size):
            if size is None:
                return
            dve.wait_ge(S["w_h"], c + 1)
            nc.vector.tensor_tensor(wL[:, s % 2, 0:size], wst[:, s, 0:size], wH[:, s % 2, 0:size].bitcast(f32),
                                    ALU.subtract).then_inc(S["w_ready"], 1)

        def gain_low(ph, k):
            if ph == "final":
                return
            dve.wait_ge(S["h_h"], k + (HB[ph] + 1))
            nc.vector.scalar_tensor_tensor(tile(hL, k), tile(xT, k), column(k, GAIN[ph]), tile(hH, k).bitcast(f32),
                                           ALU.mult, ALU.subtract).then_inc(S["h_ready"], 1)

        def low_of(ph, low, src, high, k):
            dve.wait_ge(S["h_h"], HB[ph] + k + 1)
            nc.vector.tensor_tensor(low[:, k], src[:, k], high[:, k].bitcast(f32), ALU.subtract
                                    ).then_inc(S["h_ready"], 1)

        def invert_std(ph):
            dve.wait_ge(S["std_ready"], ROUND[ph])
            me.mark(nc.vector.reciprocal(rstd[:], rstd[:]))
            me.wait()

        def ffn_in(ph):
            invert_std(ph)
            n = CHUNKS[ph] // 4
            mb, cb, fb = MB[ph], CB[ph], FB[ph]

            def body(i, last):
                for u in range(2):
                    f = i * 2 + u
                    size = NEXT_SIZE[ph] if last and u else SIZE[ph]
                    for v in range(2):
                        s = 2 * u + v
                        split_low(i * 4 + (cb + s + 2), (s + 2) % 4, size)
                        dve.wait_ge(S["pe_chunk"], i * 4 + (cb + s + 1))
                        nc.vector.tensor_tensor((ta, tb)[v][:], pair((2 + s) % 4), rstd[:], ALU.mult
                                                ).then_inc(S["evac"], 1)
                    dve.wait_ge(S["evac"], i * 4 + (mb + 2 * u + 6))
                    dve.wait_ge(S["silu_done"], f + (fb + 1))
                    nc.vector.tensor_tensor(tb[:], ta[:], tb[:], ALU.mult).then_inc(S["act_in"], 1)
                    dve.wait_ge(S["act_h"], f + (fb + 1))
                    nc.vector.tensor_tensor(tile(actL, f), tb[:], tile(actH, f).bitcast(f32), ALU.subtract
                                            ).then_inc(S["act_ready"], 1)

            with dve.Fori(0, n - 1) as i:
                body(i, False)
            body(n - 1, True)

        def residual(ph, m, chunk, p, scale):
            if ph == "wo" and m % 2 == 0:
                dve.wait_ge(S["wo_even"], m // 2 + 1)
            else:
                dve.wait_ge(S["pe_chunk"], chunk + 1)
            if ph == "pw2":
                nx = nc.vector.scalar_tensor_tensor(tile(xT, m), pair(p), column(m, B_PW2), tile(xT, m),
                                                    ALU.add, ALU.add)
            else:
                nx = nc.vector.scalar_tensor_tensor(tile(xT, m), pair(p), scale, tile(xT, m), ALU.mult, ALU.add)
            nx.then_inc(S["x_ready"], 1)

        def ffn_out(ph):
            def body(i, last):
                c, size = i * 4 + CB[ph], NEXT_SIZE[ph] if last else SIZE[ph]
                split_low(c + 2, 2, SIZE[ph])
                residual(ph, i * 2, c + 1, 0, 0.5)
                split_low(c + 3, 3, SIZE[ph])
                split_low(c + 4, 0, size)
                gain_low(AFTER[ph], i * 2)
                residual(ph, i * 2 + 1, c + 3, 1, 0.5)
                split_low(c + 5, 1, size)
                gain_low(AFTER[ph], i * 2 + 1)

            with dve.Fori(0, 3) as i:
                body(i, False)
            body(3, True)

        nc.vector.memset(void[:], 0.0).then_inc(S["evac"], 4)
        nc.vector.memset(ones[:], 1.0)
        nc.vector.memset(eps[:], EPS).then_inc(S["consts_ready"], 1)
        dve.wait_ge(S["par_t"], 1)
        nc.vector.tensor_copy(par[:], ps[:, 0, 0:KD * NPAR].rearrange("p (k n) -> p k n", k=KD)
                              ).then_inc(S["par_ready"], 1)
        for k in range(KD):
            dve.wait_ge(S["x_t"], k + 1)
            o, p = tokens(xT, k), 1 + k % 2
            nc.vector.tensor_copy(o[:, 0:SEQ], ps[:, 2 * p, 0:SEQ])
            nc.vector.tensor_copy(o[:, SEQ:TOK], ps[:, 2 * p + 1, 0:SMP]).then_inc(S["x_ready"], 1)
        split_low(0, 0, SIZE["ffn0_in"])
        dve.wait_ge(S["par_ready"], 1)
        dve.wait_ge(S["x_ready"], KD)
        for k in range(KD):
            gain_low("ffn0_in", k)
        split_low(1, 1, SIZE["ffn0_in"])
        ffn_in("ffn0_in")
        ffn_out("ffn0_out")

        invert_std("pw1")
        me.mark(nc.vector.memset(ucat[:, :, 0:30], 0.0))
        us = ucat[:, :, 30 + SEQ:UW].rearrange("p k (b t) -> p k b t", b=NB)

        def state():
            for k in range(KD):
                dve.wait_ge(S["st_t"], k // 2 + 1)
                c = k % 2 * 240
                nc.vector.tensor_copy(us[:, k, :, 0:30],
                                      ps[:, 4 + k // 2, c:c + 240].rearrange("p (b t) -> p b t", b=NB)
                                      ).then_inc(S["st_ready"], 1)

        done = [0]

        def taps(n):
            for x in range(done[0], min(done[0] + n, CD * CW)):
                ct, k = divmod(x, CW)
                c, w, u = tokens(cT, ct)[:, 0:SEQ], column(ct, W_DW + k), ucat[:, ct, k:k + SEQ]
                if k == 0:
                    dve.wait_ge(S["u_ready"], ct + 1)
                    nx = nc.vector.tensor_scalar(c, u, w, column(ct, B_DW), ALU.mult, ALU.add)
                else:
                    me.wait()
                    nx = nc.vector.scalar_tensor_tensor(c, u, w, c, ALU.mult, ALU.add)
                if k < CW - 1:
                    me.mark(nx)
                else:
                    nx.then_inc(S["c_ready"], 1)
            done[0] += n

        dve.wait_ge(S["wd_h"], 1)
        nc.vector.tensor_tensor(wdL[:], par[:, CD:KD, W_DW:NPAR], wdH[:].bitcast(f32), ALU.subtract
                                ).then_inc(S["wd_ready"], 1)
        for ct in range(KD):
            size = NEXT_SIZE["pw1"] if ct == KD - 1 else SIZE["pw1"]
            for v in range(2):
                c = CB["pw1"] + 2 * ct + v
                split_low(c + 2, (c + 2) % 4, size)
                dve.wait_ge(S["pe_chunk"], c + 1)
                if ct and v == 0:
                    dve.wait_ge(S["u_ready"], ct)
                nc.vector.tensor_tensor((ta, tb)[v][:], pair((2 + 2 * ct + v) % 4), rstd[:], ALU.mult
                                        ).then_inc(S["evac"], 1)
                if ct == 1 and v == 0:
                    state()
                if ct:
                    taps(4 + v)
            dve.wait_ge(S["evac"], MB["pw1"] + 2 * ct + 6)
            dve.wait_ge(S["glu_done"], ct + 1)
            a, g, w = tokens(ta), tokens(tb), column(ct, B_PW1)
            nc.vector.scalar_tensor_tensor(ucat[:, ct, 30:30 + SEQ], a[:, 0:SEQ], w, g[:, 0:SEQ], ALU.add, ALU.mult)
            nc.vector.scalar_tensor_tensor(
                us[:, ct, :, 30:30 + NT], a[:, SEQ:TOK].rearrange("p (b t) -> p b t", b=NB), w,
                g[:, SEQ:TOK].rearrange("p (b t) -> p b t", b=NB), ALU.add, ALU.mult).then_inc(S["u_ready"], 1)
        dve.wait_ge(S["u_ready"], KD)
        nc.vector.tensor_copy(un[:].rearrange("p k (b t) -> p k b t", b=NB), us[:, :, :, 30:30 + NT]
                              ).then_inc(S["un_ready"], 1)
        taps(3 * CW - done[0])
        dve.wait_ge(S["uh_ready"], 3)
        nc.vector.tensor_tensor(uL[0][:], ucat[:, CD + 2, 0:30 + SEQ], uH[0][:].bitcast(f32), ALU.subtract
                                ).then_inc(S["ul7_ready"], 1)
        taps(CD * CW - done[0])
        dve.wait_ge(S["c_ready"], CD)
        dve.wait_ge(S["mu_mm"], KD)
        for k in range(KD):
            nc.vector.scalar_tensor_tensor(cT[:, k], pair(0), -1.0 / D, cT[:, k], ALU.mult, ALU.add
                                           ).then_inc(S["cc_ready"], 1)
        dve.wait_ge(S["lnstd_ready"], 1)
        me.mark(nc.vector.reciprocal(rstd[:], rstd[:]))
        me.wait()
        dve.wait_ge(S["cc_ready"], KD)
        for k in range(KD):
            nc.vector.tensor_tensor(cT[:, k], cT[:, k], rstd[:], ALU.mult).then_inc(S["ln_in"], 1)
            if k:
                low_of("pw2", cL, cT, cH, k - 1)
        low_of("pw2", cL, cT, cH, KD - 1)
        for m in range(KD):
            c = CB["pw2"] + m
            residual("pw2", m, c, m % 2, None)
            split_low(c + 2, (m + 2) % 4, SIZE["pw2"] if m < KD - 2 else NEXT_SIZE["pw2"])
            gain_low("ffn1_in", m)
        ffn_in("ffn1_in")
        ffn_out("ffn1_out")

        dve.wait_ge(S["stdT_ready"], 1)
        me.mark(nc.vector.reciprocal(rstdT[:, 0:4], rstdT[:, 0:4]))
        nc.vector.reciprocal(rstdT[0:SMP, 4:5], rstdT[0:SMP, 4:5]).then_inc(S["kv_evac"], 5)
        me.wait()
        dve.wait_ge(S["kv_evac"], 5)
        for n in range(6):
            for s in range(4):
                c = 4 * n + s + 2
                if s == 3:
                    if n >= 2:
                        dve.wait_ge(S[f"kv_out{n % 2}"], 32 * (n // 2))
                    dve.wait_ge(S["pe_chunk"], CB["kv"] + 4 * n + 4)
                    for t in range(TT):
                        r = P if t < 4 else SMP
                        nc.vector.tensor_scalar(kvst[0:r, n % 2, t, :], ps[0:r, t, :], rstdT[0:r, t:t + 1], None,
                                                ALU.mult).then_inc(S["kv_evac"], 1)
                split_low(CB["kv"] + c, c % 4, SIZE["kv"] if c < 24 else NEXT_SIZE["kv"])
        for k in range(KD):
            gain_low("ffn2_in", k)
        ffn_in("ffn2_in")
        ffn_out("ffn2_out")

        invert_std("q")
        for c in range(12):
            split_low(CB["q"] + c + 2, (c + 2) % 4, SIZE["q"] if c < 10 else None)
            dve.wait_ge(S["pe_chunk"], CB["q"] + c + 1)
            nc.vector.tensor_tensor(qT[:, c, :].rearrange("p (a b) -> p a b", a=2), pair((2 + c) % 4), rstd[:],
                                    ALU.mult).then_inc(S["evac"], 1)
        dve.wait_ge(S["evac"], MB["q"] + 12 + 4)

        dve.wait_ge(S["evac"], 4)
        nc.vector.memset(void[:, 0:1], 0.0).then_inc(S["s_evac"], 1)
        nc.vector.memset(void[:, 1:2], 0.0).then_inc(S["o_evac"], 2)

        def keys(j):
            dve.wait_ge(S["kt_tr"], j * 3 + 2)
            nc.vector.tensor_copy(kT[:, 4:8, :].rearrange("p x n -> p (x n)"), ps[:, 7, :]).then_inc(S["kt_d"], 1)

        def bias_max(j, u, first=False):
            r, h2, o, c = u % 8 // 2, u % 2, u % 2, u % 8
            if not first:
                dve.wait_ge(S["pt_done"], j * 8 + (u - 1))
            if c < 2:
                dve.wait_ge(S[f"b_in{h2}"], j * 48 + (u // 8 * 48 + 48))
            dve.wait_ge(S["s_done"], j * 8 + (u + 1))
            nc.vector.scalar_tensor_tensor(sP[:, o, 0:SEQ], ps[:, 2 * o, :], HD ** -0.5,
                                           bT[:, h2, 3 - r:3 - r + SEQ], ALU.mult, ALU.add)
            nc.vector.scalar_tensor_tensor(sP[:, o, SEQ:768], ps[:, 2 * o + 1, 0:256], HD ** -0.5,
                                           bT[:, h2, T0W:], ALU.mult, ALU.add).then_inc(S["s_evac"], 1)
            dve.wait_ge(S["s_evac"], j * 8 + (u + 2))
            me.mark(nc.vector.reduce_max(stat[:, 16 + c:17 + c], sP[:, o, :], AX.X))
            me.wait()
            nc.vector.tensor_scalar(stat[:, c:c + 1], stat[:, 16 + c:17 + c], -1.0, None, ALU.mult
                                    ).then_inc(S["sm_ready"], 1)

        def prompt_pair(j, last):
            for u in range(8):
                if u < 6 or not last:
                    bias_max(j, u + 2)
                o = u % 2
                dve.wait_ge(S["pv_done"], j * 8 + (u + 3))
                me.mark(nc.vector.reciprocal(stat[:, 24 + u:25 + u], stat[:, 8 + u:9 + u]))
                me.wait()
                nc.vector.tensor_scalar(oS[:, u // 2, HD * o:HD * (o + 1)], ps[:, 6, HD * o:HD * (o + 1)],
                                        stat[:, 24 + u:25 + u], None, ALU.mult).then_inc(S["o_evac"], 1)
                if u == 5 and not last:
                    keys(j + 1)
                    pair_queries(nc.vector.tensor_copy, j + 1, 1).then_inc(S["qc_d"], 1)
            dve.wait_ge(S["ot_done"], j + 1)
            ot = tokens(oT, j)[:, 0:SEQ].rearrange("p (a r) -> p r a", r=4)
            nc.vector.tensor_copy(ot, ps[:, 7, :].rearrange("p (r a) -> p r a", r=4)[:, :, ::-1]
                                  ).then_inc(S["ot_ready"], 1)

        dve.wait_ge(S["qc_zero"], 1)
        pair_queries(nc.vector.tensor_copy, 0, 1).then_inc(S["qc_d"], 1)
        keys(0)
        bias_max(0, 0, first=True)
        bias_max(0, 1, first=True)
        with dve.Fori(0, PAIRS - 1) as j:
            me.loop(j, 16)
            prompt_pair(j, False)
            me.end(PAIRS - 1)
        prompt_pair(PAIRS - 1, True)

        me.mark(nc.vector.memset(qs[:], 0.0))

        oTf = oT[:].rearrange("p j a b -> p j (a b)")

        def queries(i, u):
            for h2 in range(2):
                q = slice(HD * h2, HD * (h2 + 1))
                nx = nc.vector.tensor_copy(qs[q, :, NT * h2:NT * (h2 + 1)],
                                           qT[q, :, bass.ds(i * (2 * NT) + (SEQ + NT * u), NT)])
            nx.then_inc(S["q_ready"], 1)

        def kt_copies(i, u):
            for g in (4, 5, 6, 7, 10, 11):
                dve.wait_ge(S["ktr"], i * 24 + (12 * u + g + 1))
                jj, x = divmod(g, 3)
                a, n = ((C1, 512), (C2, 512), (C0, SC - C0))[x]
                nc.vector.tensor_copy(kTs[:, jj, a:a + n], ps[:, (3, 4, 5, 7)[g % 4], 0:n]).then_inc(S["ktd"], 1)

        def sample_body(i, last):
            for u in range(2):
                dve.wait_ge(S["ss_mm"], i * 2 + (u + 1))
                nc.vector.scalar_tensor_tensor(sS[:, 0:C0], ps[:, 0:2, :].rearrange("p a b -> p (a b)"), HD ** -0.5,
                                               sbias[:, 0:C0], ALU.mult, ALU.add)
                me.mark(nc.vector.scalar_tensor_tensor(sS[:, C0:SC], ps[:, 2, 0:SC - C0], HD ** -0.5, sbias[:, C0:SC],
                                                       ALU.mult, ALU.add))
                me.wait()
                me.mark(nc.vector.reduce_max(stS[:, 2:3], sS[:], AX.X))
                me.wait()
                nc.vector.tensor_scalar(stS[:, 0:1], stS[:, 2:3], -1.0, None, ALU.mult).then_inc(S["sm2"], 1)
                if not (last and u):
                    queries(i, u + 1)
                    kt_copies(i, u + 1)
                dve.wait_ge(S["p2"], i * 2 + (u + 1))
                me.mark(nc.vector.reciprocal(stS[:, 3:4], stS[:, 1:2]))
                dve.wait_ge(S["ptr_mm"], i * 6 + (3 * u + 3))
                nc.vector.tensor_copy(ptS[:, 8, :], ps[:, 5, 0:P])
                nc.vector.tensor_copy(ptS[0:24, 9, :], ps[0:24, 5, P:2 * P]).then_inc(S["ptr_d"], 1)
                dve.wait_ge(S["pv2"], i * 2 + (u + 1))
                me.wait()
                nc.vector.tensor_scalar(oSs[:], ps[:, 6, 0:P], stS[:, 3:4], None, ALU.mult).then_inc(S["os_ready"], 1)
                dve.wait_ge(S["ot2"], i * 2 + (u + 1))
                for h2 in range(2):
                    q = slice(HD * h2, HD * (h2 + 1))
                    o = oTf[q, :, bass.ds(i * (2 * NT) + (SEQ + NT * u), NT)]
                    nx = nc.vector.tensor_copy(o, ps[q, 6, 2 * P:3 * P].rearrange("p (j x) -> p j x", j=PAIRS)[
                        :, :, NT * h2:NT * (h2 + 1)])
                nx.then_inc(S["o2"], 1)

        dve.wait_ge(S["sbias_in"], 16)
        me.wait()
        queries(0, 0)
        kt_copies(0, 0)
        with dve.Fori(0, NB // 2 - 1) as i:
            me.loop(i, 6)
            sample_body(i, False)
            me.end(NB // 2 - 1)
        sample_body(NB // 2 - 1, True)
        for c in range(2):
            split_low(CB["wo"] + c, c, SIZE["wo"])
        dve.wait_ge(S["o2"], NB)
        for k in range(PAIRS):
            low_of("wo", oL, oT, oH, k)
        for m in range(KD):
            residual("wo", m, CB["wo"] + m // 2, m % 2, 1.0)
            if m % 2 == 1:
                c = m // 2 + 2
                split_low(CB["wo"] + c, c % 4, SIZE["wo"] if c < 4 else NEXT_SIZE["wo"])
            gain_low("ffn3_in", m)
        ffn_in("ffn3_in")
        ffn_out("ffn3_out")

        dve.wait_ge(S["stdT_ready"], 2)
        me.mark(nc.vector.reciprocal(rstdT[:, 0:4], rstdT[:, 0:4]))
        me.mark(nc.vector.reciprocal(rstdT[0:SMP, 4:5], rstdT[0:SMP, 4:5]))
        me.wait()
        me.wait(1)
        for t in range(TT):
            r = P if t < 4 else SMP
            dve.wait_ge(S["yt"], t + 1)
            if t >= 2:
                dve.wait_ge(S[f"y_out{t % 2}"], 16 * (t // 2))
            nc.vector.tensor_scalar(yst[0:r, t % 2, :], ps[0:r, 2 * (t % 2):2 * (t % 2) + 2, :].rearrange(
                "p a b -> p (a b)"), rstdT[0:r, t:t + 1], None, ALU.mult).then_inc(S["y_ready"], 1)

    @block.tensor
    def _(pe):
        def split_mm(outs, wh, wl, xh, xl, start, stop):
            for a, b, first in ((wh, xh, True), (wh, xl, False), (wl, xh, False)):
                for t in range(2):
                    nx = nc.tensor.matmul(outs[t], a, b[:, t, :], start=start and first,
                                          stop=stop and b is xh and not first)
            return nx

        def halves(p):
            return [ps[:, 2 * p + t, 0:HALF] for t in range(2)]

        def square_sum():
            for t in range(2):
                nx = nc.tensor.matmul(ps[:, 2 + t, 0:HALF], ones[:], tb[:, t, :], start=True, stop=True)
            return nx

        def square_sum_tokens():
            t_ = tokens(tb)
            for t in range(TT):
                r = P if t < 4 else SMP
                nx = nc.tensor.matmul(ps[0:r, 6, t:t + 1], t_[:, t * P:t * P + r], ones[:, 0:1], start=True, stop=True)
            nx.then_inc(S["ssT_done"], 1)

        def in_phase(ph, before_last=None):
            n, cb, mb = CHUNKS[ph] // 4, CB[ph], MB[ph]

            def body(i, first):
                for s in range(4):
                    if first and s == 3 and before_last:
                        before_last()
                    pe.wait_ge(S["w_ready"], i * 4 + (cb + s + 1))
                    pe.wait_ge(S["evac"], i * 4 + (mb + s + 1))
                    if first and s == 3:
                        pe.wait_ge(S["std_ready"], ROUND[ph])
                    for k in range(KD):
                        if first and s == 0:
                            pe.wait_ge(S["h_ready"], HB[ph] + k + 1)
                        nx = split_mm(halves((2 + s) % 4), wH[:, s % 2, k * P:(k + 1) * P],
                                      wL[:, s % 2, k * P:(k + 1) * P], hH[:, k], hL[:, k], k == 0, k == KD - 1)
                    nx.then_inc(S["pe_chunk"], 1)
                    if first and s == 0:
                        pe.wait_ge(S["sq_ready"], XV[ph] + 1)
                        square_sum().then_inc(S["ss_done"], 1)

            body(0, True)
            if before_last:
                pe.wait_ge(S["st_ready"], KD)
            with pe.Fori(1, n) as i:
                body(i, False)

        def out_phase(ph, fph):
            def body(i):
                for s in range(4):
                    u, v = divmod(s, 2)
                    pe.wait_ge(S["w_ready"], i * 4 + (CB[ph] + s + 1))
                    if v == 0:
                        pe.wait_ge(S["evac"], MB[ph] + 3 + u)
                        pe.wait_ge(S["x_ready"], i * 2 + (KD * XV[AFTER[ph]] + u - 1))
                    for k in range(KF // 2):
                        kf = v * (KF // 2) + k
                        if kf in (0, KF - 2, KF - 1):
                            pe.wait_ge(S["act_ready"], FB[fph] + (KF - 2 if kf == 0 else kf + 1))
                        nx = split_mm(halves(u), wH[:, s % 2, k * P:(k + 1) * P], wL[:, s % 2, k * P:(k + 1) * P],
                                      actH[:, kf], actL[:, kf], kf == 0, kf == KF - 1)
                    nx.then_inc(S["pe_chunk"], 1)

            with pe.Fori(0, 4) as i:
                body(i)

        pe.wait_ge(S["ident_ready"], 1)
        pe.wait_ge(S["consts_ready"], 1)
        pe.wait_ge(S["par_in"], 16 * 9)
        for k in range(KD):
            nx = nc.tensor.transpose(ps[:, 0, k * NPAR:(k + 1) * NPAR], parR[:, k * P:(k + 1) * P],
                                     ident[0:NPAR, 0:NPAR])
        nx.then_inc(S["par_t"], 1)
        for k in range(KD):
            if k % 4 == 0:
                pe.wait_ge(S[f"x_in{k // 4}"], 32)
            p = 1 + k % 2
            if k >= 2:
                pe.wait_ge(S["x_ready"], k - 1)
            for t in range(4):
                nc.tensor.transpose(ps[:, 2 * p, t * P:(t + 1) * P], xr[:, t, k * P:(k + 1) * P], ident[:])
            nc.tensor.transpose(ps[:, 2 * p + 1, 0:SMP], xr[0:SMP, 4, k * P:(k + 1) * P], ident[0:SMP, 0:SMP]
                                ).then_inc(S["x_t"], 1)
        in_phase("ffn0_in")
        out_phase("ffn0_out", "ffn0_in")

        def state_tiles():
            pe.wait_ge(S["st_in"], 16)
            pe.wait_ge(S["evac"], MB["pw1"] + 2 + 4)
            for k in range(KD):
                for h in range(2):
                    c = k % 2 * 240 + h * 120
                    nx = nc.tensor.transpose(ps[:, 4 + k // 2, c:c + 120], stR[:, h, k * P:(k + 1) * P],
                                             ident[0:120, 0:120])
                if k % 2:
                    nx.then_inc(S["st_t"], 1)

        in_phase("pw1", before_last=state_tiles)
        pe.wait_ge(S["evac"], MB["pw1"] + 16 + 4)

        def convolve(n):
            o = n % 2
            pe.wait_ge(S["uh_ready"], n + 1)
            pe.wait_ge(S["diag_h"], n + 1)
            if n < 2:
                pe.wait_ge(S["diag_l"], n + 1)
                pe.wait_ge(S["ul_ready"], n + 1)
            else:
                pe.wait_ge(S["ul7_ready"], 1)
            for k in range(CW):
                h, l, x, y = diagH[o][:, k, :], diagL[o][:, k, :], uH[o][:, k:k + SEQ], uL[o][:, k:k + SEQ]
                nc.tensor.matmul(ps[:, 2 + n, :], h, x, start=k == 0, stop=False)
                nc.tensor.matmul(ps[:, 2 + n, :], h, y, start=False, stop=False)
                nx = nc.tensor.matmul(ps[:, 2 + n, :], l, x, start=False, stop=k == CW - 1)
            nx.then_inc(S["conv_mm"], 1)

        def mean_of(k, last=False):
            if k < CD:
                pe.wait_ge(S["c_ready"], k + 1)
            else:
                pe.wait_ge(S["cp_ready"], k - CD + 1)
            pe.wait_ge(S["cs_ready"], k // 4 + 1)
            for t in range(2):
                nx = nc.tensor.matmul(ps[:, t, 0:HALF], ones[:], cT[:, k, t, :], start=k == 0, stop=last)
            nx.then_inc(S["mu_mm"], 1)

        convolve(0)
        mean_of(0)
        mean_of(1)
        convolve(1)
        convolve(2)
        mean_of(2)
        pe.wait_ge(S["un_ready"], 1)
        pe.wait_ge(S["cp_ready"], CP)
        for n in range(4):
            for k in range(4):
                kk = n % 2 * 4 + k
                if n < 2:
                    nx = nc.tensor.transpose(ps[0:30, 4 + n, k * P:(k + 1) * P], ucat[:, kk, SEQ:SEQ + 30], ident[:])
                else:
                    nx = nc.tensor.transpose(ps[0:SMP, 4 + n, k * P:(k + 1) * P], un[:, kk], ident[:])
            nx.then_inc(S["u_t"], 1)
        mean_of(3)
        for k in range(CD, KD):
            mean_of(k)
        pe.wait_ge(S["sel_ready"], 1)
        pe.wait_ge(S["u_ev"], 4)
        for n in range(3):
            a, b = n * 512, min(R_LEN, (n + 1) * 512)
            nx = nc.tensor.matmul(ps[0:24, 4 + n, 0:b - a], relE[:], E1[:, a:b], start=True, stop=True)
        nx.then_inc(S["b_mm"], 1)
        mean_of(CD - 1, last=True)

        def sample_bias(out, a, b, g, step=1):
            for tg in range(2):
                nc.tensor.matmul(out, sel[:, tg, g, :], E2[:, tg, a:b:step], start=tg == 0, stop=False)
            return nc.tensor.matmul(out, selm[:], Ebad[:, a:b:step], start=False, stop=True)

        sample_bias(ps[:, 7, :], C1, C2, 1)
        for k in range(KD):
            pe.wait_ge(S["csq_ready"], k + 1)
            for t in range(2):
                nx = nc.tensor.matmul(ps[:, 2 + t, 0:HALF], ones[:], (ta, tb)[k % 2][:, t, :], start=k == 0,
                                      stop=k == KD - 1)
            nx.then_inc(S["var_mm"], 1)
        pe.wait_ge(S["b_ev"], 3)
        sample_bias(ps[:, 4, :], C2, C0, 2)
        sample_bias(ps[:, 5, 0:P], C0, CN, 0)
        for g in range(3):
            nx = sample_bias(ps[:, 5, P + g:SC - C0:3], CN + g, SC, g, 3)
        nx.then_inc(S["b_mm"], 1)
        for m in range(KD):
            pe.wait_ge(S["w_ready"], CB["pw2"] + m + 1)
            if m >= 2:
                pe.wait_ge(S["x_ready"], KD * 2 + m - 1)
            if m == 1:
                pe.wait_ge(S["lnstd_ready"], 1)
            for k in range(KD):
                if m == 0:
                    pe.wait_ge(S["h_ready"], HB["pw2"] + k + 1)
                nx = split_mm(halves(m % 2), wH[:, m % 2, k * P:(k + 1) * P], wL[:, m % 2, k * P:(k + 1) * P],
                              cH[:, k], cL[:, k], k == 0, k == KD - 1)
            nx.then_inc(S["pe_chunk"], 1)

        in_phase("ffn1_in")
        out_phase("ffn1_out", "ffn1_in")

        pe.wait_ge(S["sq_ready"], XV["kv"] + 1)
        square_sum_tokens()
        for k in range(KD):
            pe.wait_ge(S["h_ready"], HB["kv"] + k + 1)
        hHf, hLf = hH[:].rearrange("p k a b -> p k (a b)"), hL[:].rearrange("p k a b -> p k (a b)")
        with pe.Fori(0, 6) as n:
            for s in range(4):
                pe.wait_ge(S["w_ready"], n * 4 + (CB["kv"] + s + 1))
                for t in range(TT):
                    r = P if t < 4 else SMP
                    if s == 0:
                        pe.wait_ge(S["kv_evac"], n * 5 + (t + 1))
                    for k2 in range(2):
                        k = 2 * s + k2
                        xh, xl = hHf[:, k, t * P:t * P + r], hLf[:, k, t * P:t * P + r]
                        a, b = wH[:, s % 2, k2 * AW:(k2 + 1) * AW], wL[:, s % 2, k2 * AW:(k2 + 1) * AW]
                        nc.tensor.matmul(ps[0:r, t, :], xh, a, start=k == 0, stop=False)
                        nc.tensor.matmul(ps[0:r, t, :], xh, b, start=False, stop=False)
                        nx = nc.tensor.matmul(ps[0:r, t, :], xl, a, start=False, stop=k == KD - 1)
                nx.then_inc(S["pe_chunk"], 1)
        pe.wait_ge(S["kv_evac"], 35)

        in_phase("ffn2_in")
        out_phase("ffn2_out", "ffn2_in")

        in_phase("q")

        pe.wait_ge(S["evac"], MB["q"] + 12 + 4)
        def keys(j, g):
            if g == 0:
                pe.wait_ge(S["k_in"], j * 48 + 48)
            elif g == 1:
                pe.wait_ge(S["kt_a"], j * 2 + 1)
            else:
                pe.wait_ge(S["kt_d"], j + 1)
            for x in range(4):
                nx = nc.tensor.transpose(ps[:, 7, x * P:(x + 1) * P], kin[:, 4 * g + x, :], ident[:])
            nx.then_inc(S["kt_tr"], 1)

        def scores(j, u, first=False):
            r, h2, o = u % 8 // 2, u % 2, u % 2
            if not first:
                pe.wait_ge(S["s_evac"], j * 8 + u)
            if u % 8 == 0:
                pe.wait_ge(S["qc_a"], j + (u // 8 + 1))
                pe.wait_ge(S["kt_d"], j + (u // 8 + 1))
                pe.wait_ge(S["kt_a"], j * 2 + (u // 8 * 2 + 2))
            if u % 8 == 1:
                pe.wait_ge(S["qc_d"], j + (u // 8 + 1))
            nc.tensor.matmul(ps[:, 2 * o, :], qc[:, h2, 0, r, :], kT[:, 0:4, :].rearrange("p x n -> p (x n)"),
                             start=True, stop=True)
            for g in (1, 2):
                nx = nc.tensor.matmul(ps[:, 2 * o + 1, (g - 1) * P:g * P], qc[:, h2, g, r, :], kT[:, 4 * g + r, :],
                                      start=True, stop=True)
            nx.then_inc(S["s_done"], 1)

        def prompt_pair(j, last):
            for u in range(8):
                r, h2, o = u // 2, u % 2, u % 2
                pe.wait_ge(S["p_ready"], j * 8 + (u + 1))
                for x in range(6):
                    nx = nc.tensor.transpose(ps[:, 4 + x // 4, x % 4 * P:(x % 4 + 1) * P],
                                             sP[:, o, x * P:(x + 1) * P], ident[:])
                nx.then_inc(S["pt_done"], 1)
                if u < 6 or u == 7 and not last:
                    scores(j, u + 2)
                if u in (5, 6) and not last:
                    keys(j + 1, 2 * (u - 5))
                pe.wait_ge(S["pt_ready"], j * 8 + (u + 1))
                pe.wait_ge(S["o_evac"], j * 8 + (u + 2))
                for x in range(6):
                    nx = nc.tensor.matmul(ps[:, 6, 0:P], pT[:, o, x * P:(x + 1) * P],
                                          vin[:, x if x < 4 else 4 * (x - 3) + r, bass.ds(j * P, P)],
                                          start=x == 0, stop=x == 5)
                nx.then_inc(S["pv_done"], 1)
                if u == 5 and not last:
                    keys(j + 1, 1)
                if u == 6 and not last:
                    scores(j, 8)
            pe.wait_ge(S["o_evac"], j * 8 + 10)
            for r in range(4):
                nx = nc.tensor.transpose(ps[:, 7, r * P:(r + 1) * P], oS[:, r, :], ident[:])
            nx.then_inc(S["ot_done"], 1)

        nc.tensor.transpose(ps[:, 0, 0:P], ident[:], ident[:]).then_inc(S["pv_done"], 2)
        for g in range(3):
            keys(0, g)
        scores(0, 0, first=True)
        scores(0, 1, first=True)
        pe.wait_ge(S["v_in"], 48)
        with pe.Fori(0, PAIRS - 1) as j:
            prompt_pair(j, False)
        prompt_pair(PAIRS - 1, True)

        def transposes(i, u):
            o = u % 2
            pe.wait_ge(S[f"kc_in{o}"], (i + u // 2) * 112 + 112)
            for g in range(12):
                j, x = divmod(g, 3)
                bank = (3, 4, 5, 7)[g % 4]
                if 4 <= g < 8:
                    pe.wait_ge(S["kta"], i * 12 + (6 * u + g - 3))
                elif g >= 8:
                    pe.wait_ge(S["ktd"], i * 12 + (6 * u + g - 7))
                cols = slice(j * P, (j + 1) * P)
                if x < 2:
                    for k in range(4):
                        nx = nc.tensor.transpose(ps[:, bank, k * P:(k + 1) * P], kc[o][:, 4 * x + k, cols], ident[:])
                else:
                    nc.tensor.transpose(ps[:, bank, 0:P], kc[o][:, 8, cols], ident[:])
                    nx = nc.tensor.transpose(ps[:, bank, P:P + 24], kn[o][:, cols], ident[0:24, 0:24])
                nx.then_inc(S["ktr"], 1)

        def sample_body(i, last):
            for u in range(2):
                pe.wait_ge(S["q_ready"], i * 2 + (u + 1))
                pe.wait_ge(S["ktd"], i * 12 + (6 * u + 6))
                pe.wait_ge(S["kta"], i * 12 + (6 * u + 6))
                for bank, g, a, b, c, step in (
                        (0, 1, C1, C2, 0, 1), (1, 2, C2, C0, 0, 1), (2, 0, C0, CN, 0, 1),
                        (2, 0, CN, SC, P, 3), (2, 1, CN + 1, SC, P + 1, 3), (2, 2, CN + 2, SC, P + 2, 3)):
                    for j in range(PAIRS):
                        nx = nc.tensor.matmul(ps[32 * j:32 * j + 32, bank, c:c + b - a:step], qs[:, 4 * g + j, :],
                                              kTs[:, j, a:b:step], start=True, stop=True, tile_position=(0, 32 * j))
                nx.then_inc(S["ss_mm"], 1)
                if not (last and u):
                    transposes(i, u + 1)
                pe.wait_ge(S["p2"], i * 2 + (u + 1))
                if not (last and u):
                    pe.wait_ge(S["ktd"], i * 12 + (6 * u + 12))
                    pe.wait_ge(S["kta"], i * 12 + (6 * u + 12))
                for k in range(10):
                    n = P if k < 9 else 24
                    nx = nc.tensor.transpose(ps[0:n, 3 + k // 4, k % 4 * P:(k % 4 + 1) * P], sS[:, k * P:k * P + n],
                                             ident[:])
                    if k in (3, 7, 9):
                        nx.then_inc(S["ptr_mm"], 1)
                pe.wait_ge(S[f"vc_in{u}"], i * 112 + 112)
                pe.wait_ge(S["ptr_a"], i * 4 + (2 * u + 2))
                pe.wait_ge(S["ptr_d"], i * 2 + (u + 1))
                for k in range(10):
                    n = P if k < 9 else 24
                    for j in range(PAIRS):
                        cols = slice(j * P, (j + 1) * P)
                        a = vc[u][:, k, cols] if k < 9 else vn[u][:, cols]
                        nx = nc.tensor.matmul(ps[32 * j:32 * j + 32, 6, 0:P], ptS[0:n, k, 32 * j:32 * j + 32], a,
                                              start=k == 0, stop=k == 9, tile_position=(0, 32 * j))
                nx.then_inc(S["pv2"], 1)
                pe.wait_ge(S["os_ready"], i * 2 + (u + 1))
                nc.tensor.transpose(ps[:, 6, 2 * P:3 * P], oSs[:], ident[:]).then_inc(S["ot2"], 1)

        pe.wait_ge(S["ot_ready"], PAIRS)
        transposes(0, 0)
        with pe.Fori(0, NB // 2 - 1) as i:
            sample_body(i, False)
        sample_body(NB // 2 - 1, True)

        for m in range(KD):
            s = m // 2
            pe.wait_ge(S["w_ready"], CB["wo"] + s + 1)
            if m >= 2:
                pe.wait_ge(S["x_ready"], KD * XV["ffn3_in"] + m - 1)
            for k in range(PAIRS):
                if m == 0:
                    pe.wait_ge(S["h_ready"], HB["wo"] + k + 1)
                cols = slice(k * 2 * P + m % 2 * P, k * 2 * P + m % 2 * P + P)
                nx = split_mm(halves(m % 2), wH[:, s % 2, cols], wL[:, s % 2, cols], oH[:, k], oL[:, k], k == 0,
                              k == PAIRS - 1)
            nx.then_inc(S["wo_even" if m % 2 == 0 else "pe_chunk"], 1)

        in_phase("ffn3_in")
        out_phase("ffn3_out", "ffn3_in")

        pe.wait_ge(S["sq_ready"], XV["final"] + 1)
        square_sum_tokens()
        pe.wait_ge(S["yg_ready"], KD)
        pe.wait_ge(S["x_ready"], KD * 7)
        ygf = yg[:].rearrange("p k a b -> p k (a b)")
        for t in range(TT):
            r = P if t < 4 else SMP
            if t >= 2:
                pe.wait_ge(S["y_ready"], t - 1)
            for k in range(KD):
                nx = nc.tensor.transpose(ps[0:r, 2 * (t % 2) + k // 4, k % 4 * P:(k % 4 + 1) * P],
                                         ygf[:, k, t * P:t * P + r], ident[:])
            nx.then_inc(S["yt"], 1)

    block_cm.__exit__(None, None, None)


_OUTS = (("y_prompt", (1, SEQ, D)), ("y_sample", (NB, NT, D)), ("conv_prompt", (1, 1, CW - 1, D)),
         ("conv_sample", (1, NB, CW - 1, D)), ("kv0_prompt", (1, 128, 2, HEADS, HD)),
         ("kv0_sample", (NB, 128, 2, HEADS, HD)), ("kv1_prompt", (1, SEQ, 2, HEADS, HD)),
         ("kv1_sample", (NB, 512, 2, HEADS, HD)), ("kv2_prompt", (1, SEQ, 2, HEADS, HD)),
         ("kv2_sample", (NB, PAST, 2, HEADS, HD)))


def kernel(**inputs):
    import concourse.bacc as bacc
    from concourse.bass_utils import run_bass_kernel_spmd

    nc = bacc.Bacc("TRN2", target_bir_lowering=False, num_devices=1)
    given = {name: np.ascontiguousarray(a) for name, a in inputs.items()}
    given.update(zip(("onehot", "onehot_sample", "unseen_sample", "unseen_rows"), bias_onehots()))
    ins = {n: nc.dram_tensor(f"in_{n}", a.shape, mybir.dt.from_np(a.dtype), kind="ExternalInput").ap()
           for n, a in given.items()}
    outs = {n: nc.dram_tensor(f"out_{n}", shape, f32, kind="ExternalOutput").ap() for n, shape in _OUTS}
    trunk_program(nc, ins, outs)
    r = run_bass_kernel_spmd(nc, [{f"in_{n}": a for n, a in given.items()}], core_ids=[0])
    return tuple(r.results[0][f"out_{n}"] for n, _ in _OUTS)
```
